# Optimizing a Trainium2 kernel written in Bass

```python
import math
import jax, jax.numpy as jnp
from jax import lax
import numpy as np

D_MODEL = 1024
BATCH = 1
SEQ = 512
DEPTH = 2

CHUNK = 64
Q_BLOCK = 128
HEAD_DIM = 64
SB_HEADS = 8
SW_Q_HEADS = 8
SW_KV_HEADS = 2
SW_WINDOW = 128
SW_WINDOW_CHUNKS = SW_WINDOW // CHUNK
SB_W = SB_HEADS * HEAD_DIM
SW_Q_W = SW_Q_HEADS * HEAD_DIM
SW_KV_W = SW_KV_HEADS * HEAD_DIM
AB_IN = 3 * SB_W + SW_Q_W + 2 * SW_KV_W
AB_MIX = SB_W + SW_Q_W
HG_DK = 128
HG_HEADS = D_MODEL // HG_DK
HG_DV = D_MODEL // HG_HEADS
HG_KEY = HG_HEADS * HG_DK
HG_VAL = HG_HEADS * HG_DV
HG_IN = 2 * HG_KEY + 2 * HG_VAL
D_FF = 2816
CONV_W = 3
EPS = 1e-6
N_EVEN = (DEPTH + 1) // 2
N_ODD = DEPTH // 2

kernel_name = "chunk_causal_stickbreak_swa_hgrn2_hybrid"

def rms_norm(x, g):
    xf = x.astype(jnp.float32)
    y = xf * lax.rsqrt(jnp.mean(xf * xf, axis=-1, keepdims=True) + EPS)
    return (y * g.astype(jnp.float32)).astype(x.dtype)

def modulate(h, shift, scale):
    return h * (1 + scale[:, None, :]) + shift[:, None, :]

def alibi_slopes(n):
    return jnp.exp2(-8.0 * jnp.arange(1, n + 1, dtype=jnp.float32) / n)

def stick_breaking_attention(q, k, v):
    b, s, h, d = q.shape
    nb = s // Q_BLOCK
    qf = q.astype(jnp.float32) * (d ** -0.5)
    kf = k.astype(jnp.float32)
    vf = v.astype(jnp.float32)
    qb = qf.reshape(b, nb, Q_BLOCK, h, d).transpose(1, 0, 3, 2, 4)
    key_pos = jnp.arange(s)

    def block(args):
        qblk, n = args
        z = jnp.einsum('bhqd,bshd->bhqs', qblk, kf)
        q_pos = n * Q_BLOCK + jnp.arange(Q_BLOCK)
        strict = key_pos[None, :] < q_pos[:, None]
        log_keep = jnp.where(strict, jax.nn.log_sigmoid(-z), 0.0)
        later = lax.cumsum(log_keep, axis=3, reverse=True) - log_keep
        wts = jnp.where(strict, jnp.exp(jax.nn.log_sigmoid(z) + later), 0.0)
        return jnp.einsum('bhqs,bshd->bqhd', wts, vf)

    out = lax.map(block, (qb, jnp.arange(nb)))
    return out.transpose(1, 0, 2, 3, 4).reshape(b, s, h * d)

def sliding_window_sink_attention(q, k, v, sinks):
    b, s, hq, d = q.shape
    hkv = k.shape[2]
    g = hq // hkv
    nb = s // Q_BLOCK
    qb = (q.astype(jnp.float32) * (d ** -0.5)).reshape(b, nb, Q_BLOCK, hkv, g, d)

    def band(t):
        tb = t.astype(jnp.float32).reshape(b, nb, Q_BLOCK, hkv, d)
        prev = jnp.pad(tb, ((0, 0), (1, 0), (0, 0), (0, 0), (0, 0)))[:, :-1]
        return jnp.concatenate([prev, tb], axis=2)

    kb, vb = band(k), band(v)
    logits = jnp.einsum('bnqkgd,bnskd->bnkgqs', qb, kb)
    qi = jnp.arange(Q_BLOCK)
    kj = jnp.arange(2 * Q_BLOCK)
    dist = qi[:, None] - (kj[None, :] - Q_BLOCK)
    chunk_gap = qi[:, None] // CHUNK - (kj[None, :] // CHUNK - Q_BLOCK // CHUNK)
    in_window = (chunk_gap >= 0) & (chunk_gap < SW_WINDOW_CHUNKS)
    valid = (jnp.arange(nb)[:, None, None] * Q_BLOCK + kj[None, None, :] - Q_BLOCK) >= 0
    mask = in_window[None] & valid
    slopes = alibi_slopes(hq).reshape(hkv, g)
    bias = -slopes[:, :, None, None] * jnp.abs(dist).astype(jnp.float32)
    logits = jnp.where(mask[None, :, None, None], logits + bias, -jnp.inf)
    sink = sinks.astype(jnp.float32).reshape(hkv, g)[None, None, :, :, None, None]
    m = jnp.maximum(jnp.max(logits, axis=-1, keepdims=True), sink)
    p = jnp.exp(logits - m)
    denom = jnp.sum(p, axis=-1, keepdims=True) + jnp.exp(sink - m)
    out = jnp.einsum('bnkgqs,bnskd->bnqkgd', p / denom, vb)
    return out.reshape(b, s, hq * d)

def stick_window_mixer(h, w_in, sinks, w_out):
    b, s, _ = h.shape
    proj = h @ w_in
    cuts = [int(v) for v in np.cumsum([SB_W, SB_W, SB_W, SW_Q_W, SW_KV_W])]
    sq, sk, sv, wq, wk, wv = jnp.split(proj, cuts, axis=-1)
    o_sb = stick_breaking_attention(sq.reshape(b, s, SB_HEADS, HEAD_DIM),
                                    sk.reshape(b, s, SB_HEADS, HEAD_DIM),
                                    sv.reshape(b, s, SB_HEADS, HEAD_DIM))
    o_sw = sliding_window_sink_attention(wq.reshape(b, s, SW_Q_HEADS, HEAD_DIM),
                                         wk.reshape(b, s, SW_KV_HEADS, HEAD_DIM),
                                         wv.reshape(b, s, SW_KV_HEADS, HEAD_DIM), sinks)
    o = jnp.concatenate([o_sb, o_sw], axis=-1).astype(h.dtype)
    return o @ w_out

def hgrn2_recurrence(q, k, v, log_f):
    b, s, h, dk = q.shape
    dv = v.shape[-1]
    nc = s // CHUNK

    def to_chunks(t):
        return t.reshape(b, nc, CHUNK, h, t.shape[-1]).transpose(1, 0, 3, 2, 4)

    causal = jnp.tril(jnp.ones((CHUNK, CHUNK), dtype=bool))

    def step(state, xs):
        qc, kc, vc, lfc = xs
        cum = jnp.cumsum(lfc, axis=2)
        o_inter = jnp.einsum('bhtk,bhkv->bhtv', qc * jnp.exp(cum), state)
        diff = cum[:, :, :, None, :] - cum[:, :, None, :, :]
        decay = jnp.exp(jnp.where(causal[:, :, None], diff, -jnp.inf))
        scores = jnp.einsum('bhtk,bhsk,bhtsk->bhts', qc, kc, decay)
        o = o_inter + jnp.einsum('bhts,bhsv->bhtv', scores, vc)
        last = cum[:, :, -1:, :]
        new_state = (jnp.exp(last[:, :, 0, :])[..., None] * state
                     + jnp.einsum('bhsk,bhsv->bhkv', kc * jnp.exp(last - cum), vc))
        return new_state, o

    s0 = jnp.zeros((b, h, dk, dv), jnp.float32)
    _, out = lax.scan(step, s0, (to_chunks(q), to_chunks(k), to_chunks(v), to_chunks(log_f)))
    return out.transpose(1, 0, 3, 2, 4).reshape(b, s, h, dv)

def hgrn2_mixer(h, w_in, lb, onorm_g, w_out):
    b, s, _ = h.shape
    proj = h @ w_in
    q, fr, i, g = jnp.split(proj, [HG_KEY, 2 * HG_KEY, 2 * HG_KEY + HG_VAL], axis=-1)
    lb = lb.astype(jnp.float32)
    log_f = jnp.logaddexp(jnp.log(lb), jnp.log1p(-lb) + jax.nn.log_sigmoid(fr.astype(jnp.float32)))
    k = -jnp.expm1(log_f)
    o = hgrn2_recurrence(q.astype(jnp.float32).reshape(b, s, HG_HEADS, HG_DK),
                         k.reshape(b, s, HG_HEADS, HG_DK),
                         i.astype(jnp.float32).reshape(b, s, HG_HEADS, HG_DV),
                         log_f.reshape(b, s, HG_HEADS, HG_DK))
    o = rms_norm(o, onorm_g) * jax.nn.silu(g.astype(jnp.float32).reshape(b, s, HG_HEADS, HG_DV))
    return o.reshape(b, s, HG_VAL).astype(h.dtype) @ w_out

def conv_ffn(h, w_gate, w_up, conv_w, conv_b, w_down):
    a = h @ w_gate
    a = lax.conv_general_dilated(a, conv_w[:, None, :], window_strides=(1,),
                                 padding=[(CONV_W - 1, 0)],
                                 dimension_numbers=('NWC', 'WIO', 'NWC'),
                                 feature_group_count=D_FF) + conv_b
    return (jax.nn.gelu(a) * (h @ w_up)) @ w_down

def setup_inputs(seed: int = 0) -> dict:
    key = jax.random.key(seed)
    ks = jax.random.split(key, 24)
    f32 = jnp.float32

    def nrm(k, shape, scale):
        return jax.random.normal(k, shape, f32) * scale

    return {
        "x": nrm(ks[0], (BATCH, SEQ, D_MODEL), 1.0),
        "c": nrm(ks[1], (BATCH, D_MODEL), 1.0),
        "ada_w": nrm(ks[2], (DEPTH, D_MODEL, 6 * D_MODEL), 0.5 * D_MODEL ** -0.5),
        "ada_b": nrm(ks[3], (DEPTH, 6 * D_MODEL), 0.01),
        "norm_mix_g": 1.0 + nrm(ks[4], (DEPTH, D_MODEL), 0.02),
        "norm_ffn_g": 1.0 + nrm(ks[5], (DEPTH, D_MODEL), 0.02),
        "ab_w_in": nrm(ks[6], (N_EVEN, D_MODEL, AB_IN), D_MODEL ** -0.5),
        "ab_sinks": nrm(ks[7], (N_EVEN, SW_Q_HEADS), 0.5),
        "ab_w_out": nrm(ks[8], (N_EVEN, AB_MIX, D_MODEL), AB_MIX ** -0.5),
        "hg_w_in": nrm(ks[9], (N_ODD, D_MODEL, HG_IN), D_MODEL ** -0.5),
        "hg_lb_gamma": nrm(ks[10], (DEPTH, HG_KEY), 1.0),
        "hg_onorm_g": 1.0 + nrm(ks[11], (N_ODD, HG_DV), 0.02),
        "hg_w_out": nrm(ks[12], (N_ODD, HG_VAL, D_MODEL), HG_VAL ** -0.5),
        "ffn_w_gate": nrm(ks[13], (DEPTH, D_MODEL, D_FF), D_MODEL ** -0.5),
        "ffn_w_up": nrm(ks[14], (DEPTH, D_MODEL, D_FF), D_MODEL ** -0.5),
        "ffn_conv_w": nrm(ks[15], (DEPTH, CONV_W, D_FF), CONV_W ** -0.5),
        "ffn_conv_b": nrm(ks[16], (DEPTH, D_FF), 0.01),
        "ffn_w_down": nrm(ks[17], (DEPTH, D_FF, D_MODEL), D_FF ** -0.5),
        "final_g": 1.0 + nrm(ks[18], (D_MODEL,), 0.02),
    }

def reference(x, c, ada_w, ada_b, norm_mix_g, norm_ffn_g, ab_w_in, ab_sinks, ab_w_out,
              hg_w_in, hg_lb_gamma, hg_onorm_g, hg_w_out, ffn_w_gate, ffn_w_up,
              ffn_conv_w, ffn_conv_b, ffn_w_down, final_g):
    lb_soft = jax.nn.softmax(hg_lb_gamma.astype(jnp.float32), axis=0)
    lb_all = jnp.cumsum(lb_soft, axis=0) - lb_soft[0]
    cond = jax.nn.silu(c)
    for l in range(DEPTH):
        mod = cond @ ada_w[l] + ada_b[l]
        sh1, sc1, g1, sh2, sc2, g2 = jnp.split(mod, 6, axis=-1)
        h = modulate(rms_norm(x, norm_mix_g[l]), sh1, sc1)
        j = l // 2
        if l % 2 == 0:
            y = stick_window_mixer(h, ab_w_in[j], ab_sinks[j], ab_w_out[j])
        else:
            y = hgrn2_mixer(h, hg_w_in[j], lb_all[l], hg_onorm_g[j], hg_w_out[j])
        x = x + g1[:, None, :] * y
        h = modulate(rms_norm(x, norm_ffn_g[l]), sh2, sc2)
        x = x + g2[:, None, :] * conv_ffn(h, ffn_w_gate[l], ffn_w_up[l], ffn_conv_w[l],
                                          ffn_conv_b[l], ffn_w_down[l])
    return rms_norm(x, final_g)


_drawn_inputs = setup_inputs


def setup_inputs(seed=0):
    import zlib

    import numpy as np

    out = dict(_drawn_inputs(seed))
    spreads = {}
    factors = {'ada_b': 3.217,
     'norm_mix_g': 6.092,
     'norm_ffn_g': 6.072,
     'ab_sinks': 8.0,
     'hg_onorm_g': 23.357,
     'ffn_conv_b': 8.0,
     'final_g': 8.262}
    for name, (base, spread) in spreads.items():
        noise = np.random.default_rng([zlib.crc32(name.encode()), seed]).standard_normal(out[name].shape)
        drawn = base * np.exp(spread * noise) if base else spread * noise
        out[name] = __import__('jax').numpy.asarray(drawn.astype(out[name].dtype))
    for name, factor in factors.items():
        out[name] = (out[name] * factor).astype(out[name].dtype)
    return out
```

```python
from contextlib import ExitStack

import concourse.bass as bass
import numpy as np
from concourse import mybir

F32 = mybir.dt.float32
F32R = mybir.dt.float32r
U32 = mybir.dt.uint32
ALU = mybir.AluOpType
ACT = mybir.ActivationFunctionType
AX = mybir.AxisListType

P = 128
SEQ = 512
D = 1024
DC = D // P
TB = SEQ // P
DEPTH = 2
HEAD = 64
SB_HEADS = 8
SW_HEADS = 8
SW_GROUP = 4
CHUNK = 64
HG_HEADS = 8
D_FF = 2816
FB = D_FF // P
EPS = 1e-6
NEG = -1e30
LEVELS = 7
TINY = 1e-19
MODS = 6
UNIT = 1024

SQ, SK, SV, WQ, WK, WV = 0, 4, 8, 12, 16, 17

STEPS0 = [
    ("u", SQ), ("u", SK), ("u", SV), ("A", 0), ("u", WK), ("T", 0), ("B", 0), ("u", WV), ("C", 0),
    ("A", 1), ("u", SQ + 1), ("T", 4), ("B", 1), ("u", SK + 1), ("C", 1),
    ("u", SV + 1), ("A", 2), ("u", WQ), ("T", 1), ("B", 2), ("u", WQ + 1), ("C", 2),
    ("A", 3), ("u", SQ + 2), ("B", 3), ("u", SK + 2), ("C", 3),
    ("u", SV + 2), ("A", 4), ("u", WQ + 2), ("T", 2), ("B", 4), ("u", SQ + 3), ("C", 4),
    ("A", 5), ("u", SK + 3), ("B", 5), ("u", SV + 3), ("C", 5),
    ("A", 6), ("u", WQ + 3), ("T", 3), ("B", 6), ("C", 6), ("A", 7), ("B", 7), ("C", 7),
]
UNITS0 = [b for kind, b in STEPS0 if kind == "u"]

U_IN0 = 0
U_OUT0 = U_IN0 + len(UNITS0)
U_FFN0 = U_OUT0 + DC
U_DOWN0 = U_FFN0 + 2 * FB
U_IN1 = U_DOWN0 + FB
U_OUT1 = U_IN1 + 4 * HG_HEADS
U_FFN1 = U_OUT1 + DC
U_DOWN1 = U_FFN1 + 2 * FB
U_END = U_DOWN1 + FB
HALF = FB // 2

MISC = (
    [f"small{i}" for i in range(4)]
    + ["norm0", "mod0", "mod1"]
    + [f"V{b}" for kind, b in STEPS0 if kind == "T"]
    + ["mod2", "mod3", "mod4", "mod5", "norm1", "mod6", "mod7", "mod8", "mod9", "norm2"]
    + [f"{what}{h}" for h in range(HG_HEADS) for what in ("val", "key", "diag", "kv", "osq")]
    + ["mod10", "mod11", "norm3", "norm4"]
)
MISC_AT = {name: i for i, name in enumerate(MISC)}

FREE_OUT0 = len(UNITS0) // 2
FREE0_FFN = [FREE_OUT0, FREE_OUT0 + FB + 2 * HG_HEADS]
FREE0_IN1 = FREE_OUT0 + FB
FREE1_IN1 = FREE_OUT0

Z_OFF = [0, 512, 896, 1152]
Z_LEN = [SEQ - P * j for j in range(TB)]
Z_ALL = sum(Z_LEN)


def constant_tables():
    s = np.arange(P)[:, None]
    q = np.arange(P)[None, :]
    ident = np.eye(P)
    ones = np.ones((P, P))
    suffix = np.where(s >= q, -1.0, 0.0)
    strict = np.where(s < q, 0.0, NEG)
    bands = []
    for first in (-P, 0):
        gap = s // CHUNK - (q + first) // CHUNK
        bands.append(np.where((gap >= 0) & (gap < 2), -np.abs(s - (q + first)), NEG))
    tables = np.concatenate([ident, ones, suffix, -ones, strict] + bands * 2, axis=1)
    levels = np.zeros((P, LEVELS, 2 * P))
    n = np.arange(2 * P) % 64
    for j in range(LEVELS):
        half = 1 << j
        start = (n // half) * 2 * half
        levels[:, j, :] = (s >= start) & (s < start + half)
    return tables.astype(np.float32), levels.astype(np.float32)


def trunk(nc, x, c, ada_w, ada_b, norm_mix_g, norm_ffn_g, ab_w_in, ab_sinks, ab_w_out, hg_w_in,
          hg_lb_gamma, hg_onorm_g, hg_w_out, ffn_w_gate, ffn_w_up, ffn_conv_w, ffn_conv_b,
          ffn_w_down, final_g, tables, level_masks, out):
    with ExitStack() as ctx:
        def sem(name):
            return ctx.enter_context(nc.semaphore(name))

        def sb(name, shape, dt=F32, scope=ctx):
            return scope.enter_context(nc.sbuf_tensor(name, shape, dt))

        def bank(name):
            return ctx.enter_context(nc.psum_tensor(name, [P, 512], F32))

        xT = sb("xT", [P, DC, SEQ])
        hT_hi = sb("hT_hi", [P, DC, SEQ], F32R)
        hT_lo = sb("hT_lo", [P, DC, SEQ], F32R)
        w_raw = sb("w_raw", [P, 2, UNIT])
        w_hi = sb("w_hi", [P, 2, UNIT], F32R)
        w_lo = sb("w_lo", [P, 2, UNIT], F32R)
        ada_raw = sb("ada_raw", [P, 2, UNIT])
        ada_part = sb("ada_part", [P, UNIT])
        ada_sum = sb("ada_sum", [P, 4, UNIT])
        normed = sb("normed", [P, 2, SEQ + 2])
        h32 = sb("h32", [P, 2, SEQ])
        square = sb("square", [P, 2, SEQ])
        sumsq = sb("sumsq", [P, SEQ])
        rstd = sb("rstd", [P, SEQ])
        table = sb("table", [P, 2 * P])
        ident, ones = table[:, 0:P], table[:, P:2 * P]
        small = sb("small", [P, 4, 96])
        mod = sb("mod", [P, DEPTH * MODS, DC])
        scale_g = sb("scale_g", [P, 4, DC])
        cond = sb("cond", [P, 3, DC])
        lower = sb("lower", [P, 3, DC])

        with ExitStack() as s0:
            table0 = sb("table0", [P, 2 * P], F32, s0)
            suffix, minus = table0[:, 0:P], table0[:, P:2 * P]
            ident_r = sb("ident_r", [P, P], F32R, s0)
            strict_r = sb("strict_r", [P, P], F32R, s0)
            band_r = sb("band_r", [P, 4 * P], F32R, s0)
            slope_r = sb("slope_r", [P, SW_HEADS, P], F32R, s0)
            sinks = sb("sinks", [P, SW_HEADS], F32, s0)
            soft = sb("soft", [P, 2, 4, TB], F32, s0)
            with ExitStack() as start:
                x_nat = sb("x_nat", [P, TB, D], F32, start)
                table2 = sb("table2", [P, 5 * P], F32, start)
                small_nat = sb("small_nat", [P, 4, P], F32, start)
            q_sb = sb("q_sb", [P, 4, SEQ], F32, s0)
            k_sb = sb("k_sb", [P, 4, SEQ], F32, s0)
            q_sw = sb("q_sw", [P, 4, SEQ], F32, s0)
            k_sw = sb("k_sw", [P, 2, SEQ], F32, s0)
            vT0 = sb("vT0", [P, 2, SEQ], F32, s0)
            v_nat0 = sb("v_nat0", [P, TB, 5 * P], F32, s0)
            soft_a = sb("soft_a", [P, Z_ALL], F32, s0)
            weights = sb("weights", [P, Z_ALL], F32, s0)
            softplus = sb("softplus", [P, 2, Z_ALL], F32, s0)
            oT0 = sb("oT0", [P, DC, SEQ], F32, s0)
        with ExitStack() as s1:
            vT1 = sb("vT1", [P, SEQ], F32, s1)
            v_nat1 = sb("v_nat1", [P, TB, P], F32, s1)
            k_hg = sb("k_hg", [P, SEQ], F32, s1)
            q_hg = sb("q_hg", [P, SEQ], F32, s1)
            cum = sb("cum", [P, SEQ], F32, s1)
            decay = sb("decay", [P, SEQ], F32, s1)
            level_e = sb("level_e", [P, LEVELS + 1, SEQ], F32, s1)
            level_k = sb("level_k", [P, LEVELS + 1, SEQ], F32, s1)
            level_q = sb("level_q", [P, LEVELS, 2 * P], F32, s1)
            q_dec = sb("q_dec", [P, 2, SEQ], F32, s1)
            gate_o = sb("gate_o", [P, 2, SEQ], F32, s1)
            scores = sb("scores", [P, SEQ], F32, s1)
            states = sb("states", [P, 3, P], F32, s1)
            key_nat = sb("key_nat", [P, 3, P], F32, s1)
            last_dec = sb("last_dec", [P, 2, TB], F32, s1)
            masks = sb("masks", [P, LEVELS, 2 * P], F32, s1)
            oT1 = sb("oT1", [P, DC, SEQ], F32, s1)
        starts = rstd
        gated_hi, gated_lo = [], []
        for layer in range(DEPTH):
            with ExitStack() as sf:
                gated_hi.append(sb(f"gated_hi{layer}", [P, FB, SEQ], F32R, sf))
                gated_lo.append(sb(f"gated_lo{layer}", [P, FB, SEQ], F32R, sf))
        with ExitStack() as send:
            out_nat = sb("out_nat", [P, TB, D], F32, send)

        proj = [bank("proj0"), bank("proj1")]
        zb = [bank(f"z{j}") for j in range(4)]
        obank = bank("obank")
        misc = bank("misc")

        const_in = sem("const_in")
        small_in = sem("small_in")
        x_in = sem("x_in")
        masks_in = sem("masks_in")
        raw_in = [sem("raw_in0"), sem("raw_in1")]
        ada_in = [sem("ada_in0"), sem("ada_in1")]
        out_done = sem("out_done")
        hi_done = sem("hi_done")
        lo_done = sem("lo_done")
        unit_mm = sem("unit_mm")
        proj_free = [sem("proj_free0"), sem("proj_free1")]
        misc_full = sem("misc_full")
        misc_free = sem("misc_free")
        small_clear = sem("small_clear")
        act_chain = sem("act_chain")
        dve_chain = sem("dve_chain")
        pool_chain = sem("pool_chain")
        tables_ready = sem("tables_ready")
        small_ready = sem("small_ready")
        cond_exp = sem("cond_exp")
        cond_ready = sem("cond_ready")
        ada_used = sem("ada_used")
        sum_dve = sem("sum_dve")
        sum_pool = sem("sum_pool")
        mod_ready = sem("mod_ready")
        xt_full = sem("xt_full")
        x_new = sem("x_new")
        sq_done = sem("sq_done")
        ss_done = sem("ss_done")
        rstd_done = sem("rstd_done")
        normed_done = sem("normed_done")
        h_hi = sem("h_hi")
        h_lo = sem("h_lo")
        tile_ready = sem("tile_ready")
        tile_dve = sem("tile_dve")
        v_ready = sem("v_ready")
        z_full = sem("z_full")
        abs_done = sem("abs_done")
        log_done = sem("log_done")
        sp_done = sem("sp_done")
        cum_full = sem("cum_full")
        wt_done = sem("wt_done")
        pv_done = sem("pv_done")
        o_free = sem("o_free")
        sw_full = sem("sw_full")
        max_done = sem("max_done")
        p_done = sem("p_done")
        p_norm = sem("p_norm")
        pt_full = sem("pt_full")
        pt_act = sem("pt_act")
        pt_dve = sem("pt_dve")
        hv_ready = sem("hv_ready")
        hvn_ready = sem("hvn_ready")
        fexp_done = sem("fexp_done")
        f_ready = sem("f_ready")
        logf_done = sem("logf_done")
        cum_done = sem("cum_done")
        diff_done = sem("diff_done")
        dec_done = sem("dec_done")
        level_exp = sem("level_exp")
        lk_done = sem("lk_done")
        hq_ready = sem("hq_ready")
        lq_done = sem("lq_done")
        keyn_ready = sem("keyn_ready")
        lev_full = sem("lev_full")
        score_done = sem("score_done")
        state_done = sem("state_done")
        gexp_done = sem("gexp_done")
        g_done = sem("g_done")
        ho_full = sem("ho_full")
        osq_done = sem("osq_done")
        orstd_done = sem("orstd_done")
        ho_free = sem("ho_free")
        ho_done = sem("ho_done")
        ga_done = sem("ga_done")
        conv_done = sem("conv_done")
        gelu_done = sem("gelu_done")
        gp_done = sem("gp_done")
        gp_hi = sem("gp_hi")
        gp_lo = sem("gp_lo")
        fin_mul = sem("fin_mul")
        fin_y = sem("fin_y")
        fin_full = sem("fin_full")
        fin_evac = sem("fin_evac")

        bias_col = small[:, 0, 0:96]
        c_col = small[:, 1, 0:8]
        mix_g = [small[:, 1, 8 + 8 * i:16 + 8 * i] for i in range(2)]
        ffn_g = [small[:, 1, 24 + 8 * i:32 + 8 * i] for i in range(2)]
        fin_g = small[:, 1, 40:48]
        gamma = [small[:, 1, 48 + 8 * i:56 + 8 * i] for i in range(2)]
        onorm = small[:, 1, 64:65]
        norm_g = [mix_g[0], ffn_g[0], mix_g[1], ffn_g[1]]

        def conv_col(layer, tap, f):
            return small[:, 2 + layer, bass.ds(f + tap * FB, 1)]

        h_base = {"norm0": 0, "o0": 8, "norm1": 16, "norm2": 24, "o1": 32, "norm3": 40}

        def window_block(b, s):
            z = zb[2 * s + b // 2]
            lo, n = ((0, P), (P, 2 * P), (0, 2 * P), (2 * P, 2 * P))[b]
            at = (0, P, 3 * P, 5 * P)[b]
            return z, lo, at, n

        block = ctx.enter_context(nc.Block())

        @block.sync
        def _(sp):
            def slot_free(u):
                sp.wait_ge(lo_done, u - 1)

            def load(slot, dst_shape, src):
                a, b = dst_shape
                sp.dma_start(w_raw[:, slot, :].rearrange("p (a b) -> p a b", a=a, b=b),
                             src).then_inc(raw_in[slot], 16)

            def columns(w, at, n=P):
                return w[:, bass.ds(at, n)].rearrange("(k p) n -> p k n", p=P)

            def rows(dst, lo, n, src):
                sp.dma_start(small_nat[lo:lo + n, dst, :], src).then_inc(small_in, 16)

            sp.wait_ge(small_clear, 1)
            rows(1, 0, 8, c.rearrange("b (r p) -> (b r) p", p=P))
            rows(1, 48, 16, hg_lb_gamma.rearrange("l (r p) -> (l r) p", p=P))
            sp.dma_start(table[:], tables[:, 0:2 * P]).then_inc(const_in, 16)
            sp.dma_start(table0[:], tables[:, 2 * P:4 * P]).then_inc(const_in, 16)
            rows(0, 0, 96, ada_b.rearrange("l (r p) -> (l r) p", p=P))
            rows(1, 8, 16, norm_mix_g.rearrange("l (r p) -> (l r) p", p=P))
            rows(1, 24, 16, norm_ffn_g.rearrange("l (r p) -> (l r) p", p=P))
            rows(1, 40, 8, final_g.rearrange("(r p) -> r p", p=P))
            rows(1, 64, 1, hg_onorm_g)
            for layer in range(DEPTH):
                rows(2 + layer, 0, 3 * FB, ffn_conv_w[layer].rearrange("w (r p) -> (w r) p", p=P))
                rows(2 + layer, 3 * FB, FB, ffn_conv_b[layer].rearrange("(r p) -> r p", p=P))
            sp.dma_start(table2[:], tables[:, 4 * P:9 * P]).then_inc(const_in, 16)
            sp.dma_start(sinks[:], ab_sinks.partition_broadcast(P).rearrange("p a h -> p (a h)")
                         ).then_inc(const_in, 16)
            sp.dma_start(x_nat[:], x[0].rearrange("(t p) d -> p t d", p=P)).then_inc(x_in, 16)

            for u, b in enumerate(UNITS0):
                if u >= 2:
                    slot_free(u)
                load(u % 2, (DC, P), columns(ab_w_in[0], P * b))

            def out_units(u0, w):
                with sp.Fori(0, DC // 2) as i:
                    for s in range(2):
                        slot_free(u0 + 2 * i + s)
                        load(s, (DC, P), columns(w, i * (2 * P) + P * s))

            def ffn_units(layer, u0):
                with sp.Fori(0, FB) as f:
                    for s, w in enumerate((ffn_w_gate[layer], ffn_w_up[layer])):
                        slot_free(u0 + 2 * f + s)
                        load(s, (DC, P), columns(w, f * P))

            def down_units(layer, u0):
                w = ffn_w_down[layer]

                def one(n, half, slot, u):
                    slot_free(u)
                    src = w[bass.ds(n * (2 * P), 2 * P), half * 512:half * 512 + 512]
                    load(slot, (2, 512), src.rearrange("(k p) n -> p k n", p=P))

                with sp.Fori(0, HALF // 2) as i:
                    for s in range(2):
                        one(2 * i + s, 0, s, u0 + 2 * i + s)
                one(HALF - 1, 0, 0, u0 + HALF - 1)
                one(0, 1, 1, u0 + HALF)
                with sp.Fori(0, HALF // 2) as i:
                    for s in range(2):
                        one(2 * i + (1 + s), 1, s, u0 + HALF + 1 + 2 * i + s)

            out_units(U_OUT0, ab_w_out[0])
            ffn_units(0, U_FFN0)
            down_units(0, U_DOWN0)
            for h in range(HG_HEADS):
                for n, part in enumerate((2, 1, 0, 3)):
                    slot_free(U_IN1 + 4 * h + n)
                    load(n % 2, (DC, P), columns(hg_w_in[0][:, part * D:(part + 1) * D], h * P))
            out_units(U_OUT1, hg_w_out[0])
            ffn_units(1, U_FFN1)
            down_units(1, U_DOWN1)

            out_view = out[0].rearrange("(t p) d -> p t d", p=P)
            for k in range(4):
                sp.wait_ge(fin_evac, 2 * k + 2)
                sp.dma_start(out_view[:, :, 2 * k * P:(2 * k + 2) * P],
                             out_nat[:, :, 2 * k * P:(2 * k + 2) * P]).then_inc(out_done, 16)
            sp.wait_ge(out_done, 64)

        @block.gpsimd
        def _(pool):
            def load(j):
                g, k = divmod(j, DC)
                layer, which = divmod(g, MODS)
                pool.dma_start(ada_raw[:, j % 2, :],
                               ada_w[layer, k * P:(k + 1) * P, which * D:(which + 1) * D]
                               ).then_inc(ada_in[j % 2], 16)

            chain = [0]
            total = DEPTH * MODS * DC
            pool.memset(small_nat[:], 0.0).then_inc(small_clear, 1)
            for j in range(2):
                load(j)
            for j in range(2, 2 * DC + 2):
                pool.wait_ge(ada_used, j - 1)
                load(j)
            for j in range(2 * DC, total):
                g, k = divmod(j, DC)
                if g >= 4 and k == 0:
                    pool.wait_ge(misc_full, MISC_AT[f"mod{g - 4}"] + 1)
                if k == 0 and g == 2:
                    pool.wait_ge(cond_ready, 1)
                pool.wait_ge(ada_in[j % 2], 16 * (j // 2 + 1))
                acc = ada_sum[:, g % 4, :]
                scale = cond[:, 2, k:k + 1]
                if k == 0:
                    pool.tensor_scalar(acc, ada_raw[:, j % 2, :], scale, None, ALU.mult
                                       ).then_inc(pool_chain, 1)
                    chain[0] += 1
                    pool.wait_ge(pool_chain, chain[0])
                else:
                    pool.tensor_scalar(ada_part[:], ada_raw[:, j % 2, :], scale, None, ALU.mult
                                       ).then_inc(pool_chain, 1)
                    chain[0] += 1
                    pool.wait_ge(pool_chain, chain[0])
                    pool.tensor_tensor(acc, acc, ada_part[:], ALU.add).then_inc(sum_pool, 1)
                    pool.wait_ge(sum_pool, (g - 2) * (DC - 1) + k)
                if j + 2 < total:
                    load(j + 2)

            pool.wait_ge(x_new, 3 * DC)
            pool.dma_start(masks[:], level_masks.rearrange("p (j n) -> p j n", j=LEVELS)
                           ).then_inc(masks_in, 16)

            for h in range(HG_HEADS):
                pool.wait_ge(level_exp, 2 * h + 2)
                if h:
                    pool.wait_ge(lev_full, h)
                for j in (LEVELS, *range(LEVELS)):
                    pool.tensor_tensor(level_k[:, j, :], level_e[:, j, :], k_hg[:], ALU.mult
                                       ).then_inc(lk_done, 1)

        @block.scalar
        def _(act):
            chain = [0]

            def link(ins):
                chain[0] += 1
                ins.then_inc(act_chain, 1)
                act.wait_ge(act_chain, chain[0])

            def split(u, slot):
                act.wait_ge(raw_in[slot], u * 8 + (16 - 8 * slot))
                if not (isinstance(u, int) and u < 2):
                    act.wait_ge(unit_mm, u - 1)
                nc.scalar.activation(w_hi[:, slot, :], w_raw[:, slot, :], ACT.Copy).then_inc(hi_done, 1)

            def squares(n, dc):
                act.wait_ge(x_new, 8 * n + dc + 1)
                if dc > 2:
                    act.wait_ge(ss_done, 7 * n + dc - 2)
                dst = square[:, dc % 2, :] if dc else sumsq[:]
                nc.scalar.activation(dst, xT[:, dc, :], ACT.Square).then_inc(sq_done, 1)

            def root(n):
                act.wait_ge(misc_full, MISC_AT[f"norm{n}"] + 1)
                nc.scalar.activation(rstd[:], misc[:], ACT.Ln, bias=EPS, scale=1.0 / D).then_inc(misc_free, 1)
                act.wait_ge(misc_free, MISC_AT[f"norm{n}"] + 1)
                nc.scalar.activation(rstd[:], rstd[:], ACT.Exp, scale=-0.5).then_inc(rstd_done, 1)

            def modulated(n):
                base = h_base[f"norm{n}"]
                groups = 6 * (n // 2) + 3 * (n % 2)
                act.wait_ge(mod_ready, n + 1)
                for dc in range(DC):
                    act.wait_ge(normed_done, 8 * n + dc + 1)
                    if base + dc >= 2:
                        act.wait_ge(h_lo, base + dc - 1)
                    a, b = scale_g[:, n, dc:dc + 1], mod[:, groups, dc:dc + 1]
                    src = normed[:, dc % 2, 2:2 + SEQ]
                    nc.scalar.activation(h32[:, dc % 2, :], src, ACT.Identity, bias=b, scale=a)
                    nc.scalar.activation(hT_hi[:, dc, :], src, ACT.Identity, bias=b, scale=a).then_inc(h_hi, 1)

            def heads_hi(which, src, ready):
                for dc in range(DC):
                    ready(dc)
                    nc.scalar.activation(hT_hi[:, dc, :], src[:, dc, :], ACT.Copy).then_inc(h_hi, 1)

            act.wait_ge(small_ready, 4)
            nc.scalar.activation(cond[:, 0, :], c_col, ACT.Exp, scale=-1.0)
            nc.scalar.activation(lower[:, 1, :], lower[:, 0, :], ACT.Exp).then_inc(cond_exp, 1)
            for dc in range(DC):
                squares(0, dc)
            split(0, 0)
            split(1, 1)
            root(0)
            modulated(0)

            u = 0
            n_act = [0]
            for kind, b in STEPS0:
                if kind == "u":
                    split(u + 2, u % 2)
                    if b < WQ:
                        act.wait_ge(unit_mm, u + 1)
                        if SV <= b:
                            if b - SV == 2:
                                act.wait_ge(misc_full, MISC_AT["V4"] + 1)
                            if b - SV == 3:
                                act.wait_ge(misc_full, MISC_AT["V1"] + 1)
                            nc.scalar.activation(vT0[:, (b - SV) % 2, :], proj[u % 2][:], ACT.Copy
                                                 ).then_inc(proj_free[u % 2], 1)
                        elif SK <= b:
                            nc.scalar.activation(k_sb[:, b - SK, :], proj[u % 2][:], ACT.Copy
                                                 ).then_inc(proj_free[u % 2], 1)
                        else:
                            nc.scalar.activation(q_sb[:, b, :], proj[u % 2][:], ACT.Copy, scale=HEAD ** -0.5
                                                 ).then_inc(proj_free[u % 2], 1)
                    u += 1
                elif kind == "A":
                    if b:
                        act.wait_ge(sp_done, 4 * b)
                    for j in range(TB):
                        act.wait_ge(z_full, 4 * b + j + 1)
                        nc.scalar.activation(soft_a[:, Z_OFF[j]:Z_OFF[j] + Z_LEN[j]], zb[j][:, 0:Z_LEN[j]],
                                             ACT.Abs).then_inc(abs_done, 1)
                    act.wait_ge(abs_done, 4 * b + 4)
                    link(nc.scalar.activation(soft_a[:], soft_a[:], ACT.Exp, scale=-1.0))
                    nc.scalar.activation(soft_a[:], soft_a[:], ACT.Ln, bias=1.0).then_inc(log_done, 1)
                elif kind == "B":
                    if b:
                        act.wait_ge(pv_done, b)
                    for j in range(TB):
                        act.wait_ge(cum_full, 4 * b + j + 1)
                        nc.scalar.activation(weights[:, Z_OFF[j]:Z_OFF[j] + Z_LEN[j]], zb[j][:, 0:Z_LEN[j]],
                                             ACT.Exp).then_inc(wt_done, 1)
                elif kind == "T":
                    act.wait_ge(misc_full, MISC_AT[f"V{b}"] + 1)
                    nc.scalar.activation(v_nat0[:, :, b * P:(b + 1) * P],
                                         misc[:].rearrange("p (t n) -> p t n", t=TB), ACT.Copy
                                         ).then_inc(misc_free, 1)

            def window_exp(h):
                s = h % 2
                act.wait_ge(max_done, h + 1)
                p_buf = (soft_a, weights)[s]
                if h < 2:
                    act.wait_ge(pv_done, SB_HEADS)
                else:
                    act.wait_ge(pt_full, 2 * h - 2)
                for b in range(TB):
                    z, lo, at, n = window_block(b, s)
                    nc.scalar.activation(p_buf[:, at:at + n], z[:, lo:lo + n], ACT.Exp,
                                         bias=soft[:, s, 0, b:b + 1], accum_out=soft[:, s, 1, b:b + 1])
                nc.scalar.activation(soft[:, s, 2, :], soft[:, s, 0, :], ACT.Exp, bias=sinks[:, h:h + 1]
                                     ).then_inc(p_done, 1)

            def window_copy(h):
                act.wait_ge(pt_full, 2 * h + 1)
                if h >= 2:
                    act.wait_ge(pv_done, SB_HEADS + h - 1)
                nc.scalar.activation(softplus[:, h % 2, 0:384], zb[2 * (h % 2)][:, 0:384], ACT.Copy
                                     ).then_inc(pt_act, 1)

            window_exp(0)
            for h in range(SW_HEADS):
                if h + 1 < SW_HEADS:
                    window_exp(h + 1)
                window_copy(h)
            heads_hi("o0", oT0, lambda dc: act.wait_ge(o_free, dc + 1))

            def out_units(u0, n):
                for o in range(DC):
                    split(u0 + o + 2, o % 2)
                    squares(n, o)
                root(n)
                modulated(n)

            def ffn(layer, u0, base):
                with act.Fori(0, FB) as f:
                    u = u0 + 2 * f
                    split(u + 2, 0)
                    act.wait_ge(unit_mm, u + 1)
                    nc.scalar.activation(normed[:, 0, 2:2 + SEQ], proj[0][:], ACT.Copy
                                         ).then_inc(proj_free[0], 1)
                    act.wait_ge(conv_done, base + f + 1)
                    nc.scalar.activation(square[:, 1, :], square[:, 0, :], ACT.Gelu_apprx_tanh,
                                         bias=conv_col(layer, 3, f)).then_inc(gelu_done, 1)
                    split(u + 3, 1)
                    act.wait_ge(gp_done, base + f + 2)
                    nc.scalar.activation(gated_hi[layer][:, bass.ds(f, 1), :].rearrange("p a n -> p (a n)"),
                                         h32[:, 0, :], ACT.Copy).then_inc(gp_hi, 1)

            def down(u0, n, last=False):
                with act.Fori(0, HALF // 2) as i:
                    for s in range(2):
                        split(u0 + 2 * i + (2 + s), s)
                split(u0 + HALF + 1, 0)
                split(u0 + HALF + 2, 1)
                for q in range(4):
                    squares(n, q)
                with act.Fori(0, HALF // 2 - 1) as i:
                    for s in range(2):
                        split(u0 + HALF + 3 + 2 * i + s, s)
                if not last:
                    split(u0 + FB, 0)
                    split(u0 + FB + 1, 1)
                for q in range(4, DC):
                    squares(n, q)
                root(n)
                if not last:
                    modulated(n)

            out_units(U_OUT0, 1)
            ffn(0, U_FFN0, 0)
            down(U_DOWN0, 2)

            u = U_IN1
            for h in range(HG_HEADS + 1):
                p = h - 1
                if h < HG_HEADS:
                    split(u + 2, 0)
                    act.wait_ge(unit_mm, u + 1)
                    if h:
                        act.wait_ge(misc_full, MISC_AT[f"val{p}"] + 1)
                    nc.scalar.activation(vT1[:], proj[0][:], ACT.Copy).then_inc(proj_free[0], 1)
                if h:
                    act.wait_ge(misc_full, MISC_AT[f"val{p}"] + 1)
                    nc.scalar.activation(v_nat1[:], misc[:].rearrange("p (t n) -> p t n", t=TB), ACT.Copy
                                         ).then_inc(misc_free, 1)
                    act.wait_ge(misc_full, MISC_AT[f"key{p}"] + 1)
                    nc.scalar.activation(key_nat[:], misc[:, 0:384].rearrange("p (t n) -> p t n", t=3),
                                         ACT.Copy).then_inc(misc_free, 1)
                if h < HG_HEADS:
                    split(u + 3, 1)
                    act.wait_ge(unit_mm, u + 2)
                    if h:
                        act.wait_ge(cum_done, h)
                    nc.scalar.activation(normed[:, 0, 2:2 + SEQ], proj[1][:], ACT.Exp).then_inc(proj_free[1], 1)
                    act.wait_ge(f_ready, h + 1)
                    nc.scalar.activation(normed[:, 0, 2:2 + SEQ], normed[:, 0, 2:2 + SEQ], ACT.Ln).then_inc(logf_done, 1)
                    split(u + 4, 0)
                    act.wait_ge(unit_mm, u + 3)
                    if h:
                        act.wait_ge(lq_done, p + 1)
                    nc.scalar.activation(q_hg[:], proj[0][:], ACT.Copy).then_inc(proj_free[0], 1)
                    act.wait_ge(cum_done, h + 1)
                    nc.scalar.activation(decay[:], cum[:], ACT.Exp).then_inc(dec_done, 1)
                    for part in range(2):
                        act.wait_ge(diff_done, 2 * h + part + 1)
                        e = level_e[:, 4 * part:4 * part + 4, :]
                        nc.scalar.activation(e, e, ACT.Exp).then_inc(level_exp, 1)
                    split(u + 5, 1)
                    act.wait_ge(unit_mm, u + 4)
                    if h:
                        act.wait_ge(g_done, h)
                    nc.scalar.activation(normed[:, 1, 2:2 + SEQ], proj[1][:], ACT.Exp, scale=-1.0
                                         ).then_inc(gexp_done, 1)
                if h:
                    act.wait_ge(ho_full, p + 1)
                    if p:
                        act.wait_ge(misc_full, MISC_AT[f"osq{p - 1}"] + 1)
                    nc.scalar.activation(square[:, 0, :], obank[:], ACT.Square).then_inc(osq_done, 1)
                    act.wait_ge(misc_full, MISC_AT[f"osq{p}"] + 1)
                    if p:
                        act.wait_ge(ho_done, p)
                    nc.scalar.activation(square[:, 1, :], misc[:], ACT.Ln, bias=EPS, scale=1.0 / P
                                         ).then_inc(misc_free, 1)
                    act.wait_ge(misc_free, MISC_AT[f"osq{p}"] + 1)
                    nc.scalar.activation(square[:, 1, :], square[:, 1, :], ACT.Exp, scale=-0.5
                                         ).then_inc(orstd_done, 1)
                u += 4
            heads_hi("o1", oT1, lambda dc: act.wait_ge(ho_done, dc + 1))
            out_units(U_OUT1, 3)
            ffn(1, U_FFN1, FB)
            down(U_DOWN1, 4, last=True)

            for dc in range(DC):
                act.wait_ge(fin_mul, dc + 1)
                if dc >= 2:
                    act.wait_ge(fin_full, dc - 1)
                nc.scalar.activation(h32[:, dc % 2, :], normed[:, dc % 2, 2:2 + SEQ], ACT.Identity,
                                     scale=fin_g[:, dc:dc + 1]).then_inc(fin_y, 1)

        @block.vector
        def _(dve):
            chain = [0]

            def link(ins):
                chain[0] += 1
                ins.then_inc(dve_chain, 1)
                dve.wait_ge(dve_chain, chain[0])

            def split(u, slot):
                dve.wait_ge(hi_done, u + 1)
                nc.vector.tensor_tensor(w_lo[:, slot, :], w_raw[:, slot, :], w_hi[:, slot, :].bitcast(F32),
                                        ALU.subtract).then_inc(lo_done, 1)

            def add_squares(n, dc):
                if dc:
                    dve.wait_ge(sq_done, 8 * n + dc + 1)
                    if 7 * n + dc - 1:
                        dve.wait_ge(ss_done, 7 * n + dc - 1)
                    nc.vector.tensor_tensor(sumsq[:], sumsq[:], square[:, dc % 2, :], ALU.add).then_inc(ss_done, 1)

            def normalise(n):
                base = h_base[f"norm{n}"]
                dve.wait_ge(rstd_done, n + 1)
                for dc in range(DC + 1):
                    if dc < DC:
                        if dc >= 2:
                            dve.wait_ge(h_hi, base + dc - 1)
                        nc.vector.tensor_tensor(normed[:, dc % 2, 2:2 + SEQ], xT[:, dc, :], rstd[:], ALU.mult
                                                ).then_inc(normed_done, 1)
                    if dc:
                        low(base, dc - 1, h32[:, (dc - 1) % 2, :])

            def low(base, dc, src):
                dve.wait_ge(h_hi, base + dc + 1)
                nc.vector.tensor_tensor(hT_lo[:, dc, :], src, hT_hi[:, dc, :].bitcast(F32), ALU.subtract
                                        ).then_inc(h_lo, 1)

            def mod_group(g):
                dve.wait_ge(misc_full, MISC_AT[f"mod{g}"] + 1)
                nc.vector.tensor_tensor(mod[:, g, :], misc[:, 0:DC], bias_col[:, g * DC:(g + 1) * DC], ALU.add
                                        ).then_inc(misc_free, 1)
                dve.wait_ge(misc_free, MISC_AT[f"mod{g}"] + 1)
                if g % 3 == 1:
                    nc.vector.scalar_tensor_tensor(out=scale_g[:, g // 3, :], in0=mod[:, g, :], scalar=1.0,
                                                   in1=norm_g[g // 3], op0=ALU.add, op1=ALU.mult
                                                   ).then_inc(mod_ready, 1)

            dve.wait_ge(small_in, 16 * 11)
            dve.wait_ge(const_in, 64)
            for i in range(4):
                dve.wait_ge(misc_full, MISC_AT[f"small{i}"] + 1)
                nc.vector.tensor_copy(small[:, i, :], misc[:, 0:96]).then_inc(misc_free, 1)
            dve.wait_ge(misc_free, 4)
            nc.vector.tensor_copy(ident_r[:], ident).then_inc(gp_done, 1)
            nc.vector.tensor_copy(strict_r[:], table2[:, 0:P]).then_inc(small_ready, 1)
            nc.vector.tensor_copy(band_r[:], table2[:, P:5 * P]).then_inc(small_ready, 1)
            nc.vector.memset(normed[:, 0, 0:2], 0.0).then_inc(small_ready, 1)
            nc.vector.tensor_tensor(lower[:, 0, :], gamma[0], gamma[1], ALU.subtract).then_inc(small_ready, 1)
            dve.wait_ge(cond_exp, 1)
            link(nc.vector.tensor_scalar(cond[:, 1, :], cond[:, 0, :], 1.0, None, ALU.add))
            link(nc.vector.reciprocal(cond[:, 0, :], cond[:, 1, :]))
            nc.vector.tensor_tensor(cond[:, 2, :], c_col, cond[:, 0, :], ALU.mult).then_inc(cond_ready, 1)
            link(nc.vector.tensor_scalar(lower[:, 0, :], lower[:, 1, :], 1.0, None, ALU.add))
            link(nc.vector.reciprocal(lower[:, 1, :], lower[:, 0, :]))
            link(nc.vector.tensor_scalar(lower[:, 2, :], lower[:, 1, :], -1.0, 1.0, ALU.mult, ALU.add))
            for h in range(SW_HEADS):
                nc.vector.tensor_scalar(slope_r[:, h, :], ident, 2.0 ** (-8.0 * (h + 1) / SW_HEADS), None,
                                        ALU.mult).then_inc(tables_ready, 1)

            dve.wait_ge(cond_ready, 1)

            def ada_block(j):
                g, k = divmod(j, DC)
                dve.wait_ge(ada_in[j % 2], 16 * (j // 2 + 1))
                acc, raw, scale = ada_sum[:, g, :], ada_raw[:, j % 2, :], cond[:, 2, k:k + 1]
                if k == 0:
                    nc.vector.tensor_scalar(acc, raw, scale, None, ALU.mult).then_inc(ada_used, 1)
                else:
                    dve.wait_ge(ada_used, j)
                    nc.vector.scalar_tensor_tensor(out=acc, in0=raw, scalar=scale, in1=acc, op0=ALU.mult,
                                                   op1=ALU.add).then_inc(ada_used, 1)

            def x_block(dc):
                dve.wait_ge(xt_full, dc + 1)
                nc.vector.tensor_copy(xT[:, dc, :], zb[dc % 4][:]).then_inc(x_new, 1)

            for dc in range(DC):
                ada_block(dc)
                x_block(dc)
                if dc:
                    add_squares(0, dc - 1)
            add_squares(0, DC - 1)
            split(0, 0)
            split(1, 1)
            for k in range(DC):
                ada_block(DC + k)
            mod_group(0)
            mod_group(1)
            normalise(0)

            u = 0
            for kind, b in STEPS0:
                if kind == "u":
                    split(u + 2, u % 2)
                    if b >= WQ:
                        dve.wait_ge(unit_mm, u + 1)
                        src = proj[u % 2]
                        if b == WV:
                            dve.wait_ge(misc_full, MISC_AT["V0"] + 1)
                            nc.vector.tensor_copy(vT0[:, 0, :], src[:]).then_inc(proj_free[u % 2], 1)
                        elif b == WK:
                            for g in range(2):
                                for half in range(2):
                                    last = nc.vector.tensor_copy(
                                        k_sw[HEAD * half:HEAD * half + HEAD, g, :],
                                        src[HEAD * g:HEAD * g + HEAD, :])
                            last.then_inc(proj_free[u % 2], 1)
                        else:
                            nc.vector.tensor_scalar(q_sw[:, b - WQ, :], src[:], HEAD ** -0.5, None, ALU.mult
                                                    ).then_inc(proj_free[u % 2], 1)
                    u += 1
                elif kind == "A":
                    dve.wait_ge(log_done, b + 1)
                    if b >= 2:
                        dve.wait_ge(cum_full, 4 * (b - 1))
                    for j in range(TB):
                        at = slice(Z_OFF[j], Z_OFF[j] + Z_LEN[j])
                        nc.vector.scalar_tensor_tensor(out=softplus[:, b % 2, at], in0=zb[j][:, 0:Z_LEN[j]],
                                                       scalar=0.0, in1=soft_a[:, at], op0=ALU.max, op1=ALU.add
                                                       ).then_inc(sp_done, 1)
                elif kind == "C" and b % 2:
                    dve.wait_ge(pv_done, b + 1)
                    nc.vector.tensor_copy(oT0[:, b // 2, :], obank[:]).then_inc(o_free, 1)

            def window_max(h):
                s = h % 2
                for b in range(TB):
                    z, lo, _, n = window_block(b, s)
                    dve.wait_ge(sw_full, 2 * h + 1 + b // 2)
                    link(nc.vector.tensor_reduce(soft[:, s, 3, b:b + 1], z[:, lo:lo + n], AX.X, ALU.max))
                nc.vector.tensor_scalar(soft[:, s, 0, :], soft[:, s, 3, :], sinks[:, h:h + 1], -1.0,
                                        ALU.max, ALU.mult).then_inc(max_done, 1)

            def window_norm(h):
                s = h % 2
                dve.wait_ge(p_done, h + 1)
                link(nc.vector.tensor_tensor(soft[:, s, 3, :], soft[:, s, 1, :], soft[:, s, 2, :], ALU.add))
                link(nc.vector.reciprocal(soft[:, s, 2, :], soft[:, s, 3, :]))
                p_buf = (soft_a, weights)[s]
                for b in range(TB):
                    _, _, at, n = window_block(b, s)
                    nc.vector.tensor_scalar(p_buf[:, at:at + n], p_buf[:, at:at + n], soft[:, s, 2, b:b + 1],
                                            None, ALU.mult).then_inc(p_norm, 1)

            def window_copy(h):
                dve.wait_ge(pt_full, 2 * h + 2)
                if h >= 2:
                    dve.wait_ge(pv_done, SB_HEADS + h - 1)
                nc.vector.tensor_copy(softplus[:, h % 2, 384:896], zb[2 * (h % 2) + 1][:]).then_inc(pt_dve, 1)

            window_max(0)
            for h in range(SW_HEADS):
                window_norm(h)
                if h + 1 < SW_HEADS:
                    window_max(h + 1)
                window_copy(h)
                if h % 2:
                    dve.wait_ge(pv_done, SB_HEADS + h + 1)
                    nc.vector.tensor_copy(oT0[:, 4 + h // 2, :], obank[:]).then_inc(o_free, 1)
            for dc in range(DC):
                low(h_base["o0"], dc, oT0[:, dc, :])

            def out_units(u0, n, gate):
                for o in range(DC):
                    split(u0 + o + 2, o % 2)
                    if o == 0 and gate == 2:
                        mod_group(2)
                    dve.wait_ge(unit_mm, u0 + o + 1)
                    nc.vector.scalar_tensor_tensor(out=xT[:, o, :], in0=proj[o % 2][:],
                                                   scalar=mod[:, gate, o:o + 1], in1=xT[:, o, :],
                                                   op0=ALU.mult, op1=ALU.add).then_inc(x_new, 1)
                    add_squares(n, o)
                if n == 1:
                    for g in (3, 4, 5):
                        mod_group(g)
                normalise(n)

            def ffn(layer, u0, base):
                lc = chain[0]
                with dve.Fori(0, FB) as f:
                    u = u0 + 2 * f
                    split(u + 2, 0)
                    dve.wait_ge(proj_free[0], FREE0_FFN[layer] + f + 1)
                    nc.vector.tensor_scalar(square[:, 0, :], normed[:, 0, 0:SEQ], conv_col(layer, 0, f), None,
                                            ALU.mult).then_inc(dve_chain, 1)
                    dve.wait_ge(dve_chain, lc + 2 * f + 1)
                    nc.vector.scalar_tensor_tensor(out=square[:, 0, :], in0=normed[:, 0, 1:1 + SEQ],
                                                   scalar=conv_col(layer, 1, f), in1=square[:, 0, :],
                                                   op0=ALU.mult, op1=ALU.add).then_inc(dve_chain, 1)
                    dve.wait_ge(dve_chain, lc + 2 * f + 2)
                    nc.vector.scalar_tensor_tensor(out=square[:, 0, :], in0=normed[:, 0, 2:2 + SEQ],
                                                   scalar=conv_col(layer, 2, f), in1=square[:, 0, :],
                                                   op0=ALU.mult, op1=ALU.add).then_inc(conv_done, 1)
                    dve.wait_ge(unit_mm, u + 2)
                    dve.wait_ge(gelu_done, base + f + 1)
                    nc.vector.tensor_tensor(h32[:, 0, :], proj[1][:], square[:, 1, :], ALU.mult
                                            ).then_inc(gp_done, 1)
                    split(u + 3, 1)
                    dve.wait_ge(gp_hi, base + f + 1)
                    at = gated_lo[layer][:, bass.ds(f, 1), :].rearrange("p a n -> p (a n)")
                    hi = gated_hi[layer][:, bass.ds(f, 1), :].rearrange("p a n -> p (a n)")
                    nc.vector.tensor_tensor(at, h32[:, 0, :], hi.bitcast(F32), ALU.subtract
                                            ).then_inc(gp_lo, 1)
                chain[0] += 2 * FB

            def down(u0, n, gate, last=False):
                def half_out(half, u):
                    dve.wait_ge(unit_mm, u)
                    for q in range(4):
                        dc = 4 * half + q
                        nc.vector.scalar_tensor_tensor(out=xT[:, dc, :], in0=zb[q][:],
                                                       scalar=mod[:, gate, dc:dc + 1], in1=xT[:, dc, :],
                                                       op0=ALU.mult, op1=ALU.add).then_inc(x_new, 1)

                with dve.Fori(0, HALF // 2) as i:
                    for s in range(2):
                        split(u0 + 2 * i + (2 + s), s)
                split(u0 + HALF + 1, 0)
                half_out(0, u0 + HALF)
                split(u0 + HALF + 2, 1)
                for q in range(4):
                    add_squares(n, q)
                with dve.Fori(0, HALF // 2 - 1) as i:
                    for s in range(2):
                        split(u0 + HALF + 3 + 2 * i + s, s)
                if not last:
                    split(u0 + FB, 0)
                    split(u0 + FB + 1, 1)
                half_out(1, u0 + FB)
                for q in range(4, DC):
                    add_squares(n, q)

            out_units(U_OUT0, 1, 2)
            ffn(0, U_FFN0, 0)
            for g in range(6, 10):
                mod_group(g)
            down(U_DOWN0, 2, 5)
            normalise(2)

            nc.vector.memset(starts[:], 1.0).then_inc(tables_ready, 1)
            dve.wait_ge(tables_ready, SW_HEADS + 1)
            link(nc.vector.memset(starts[:].rearrange("p (t n) -> p t n", t=TB)[:, :, 0:1], 0.0))
            u = U_IN1
            for h in range(HG_HEADS + 1):
                p = h - 1
                if h < HG_HEADS:
                    split(u + 2, 0)
                    split(u + 3, 1)
                if h:
                    dve.wait_ge(misc_full, MISC_AT[f"diag{p}"] + 1)
                    nc.vector.tensor_tensor(
                        scores[:].rearrange("p (t n) -> p t n", t=TB), misc[:].rearrange("p (t n) -> p t n", t=TB),
                        ident.unsqueeze(1).to_broadcast([P, TB, P]), ALU.mult).then_inc(misc_free, 1)
                    dve.wait_ge(misc_free, MISC_AT[f"diag{p}"] + 1)
                    dve.wait_ge(lev_full, p + 1)
                    dve.wait_ge(masks_in, 16)
                    for j in range(LEVELS):
                        half = 1 << j
                        dst = scores[:].rearrange("p (b two r) -> p b two r", two=2, r=half)[:, :, 1, :]
                        src = zb[j // 2][:, 256 * (j % 2):256 * (j % 2) + 256].rearrange("p (b r) -> p b r", r=half)
                        m = masks[:, j, :].bitcast(U32).rearrange("p (b r) -> p b r", r=half)
                        if LEVELS * p + j:
                            dve.wait_ge(score_done, LEVELS * p + j)
                        nc.vector.copy_predicated(dst, m, src).then_inc(score_done, 1)
                    dve.wait_ge(misc_full, MISC_AT[f"kv{p}"] + 1)
                    link(nc.vector.tensor_copy(states[:, 0, :], misc[:, 0:P]))
                    link(nc.vector.scalar_tensor_tensor(
                        out=states[:, 1, :], in0=states[:, 0, :], scalar=last_dec[:, p % 2, 1:2],
                        in1=misc[:, P:2 * P], op0=ALU.mult, op1=ALU.add))
                    nc.vector.scalar_tensor_tensor(
                        out=states[:, 2, :], in0=states[:, 1, :], scalar=last_dec[:, p % 2, 2:3],
                        in1=misc[:, 2 * P:3 * P], op0=ALU.mult, op1=ALU.add).then_inc(misc_free, 1)
                if h < HG_HEADS:
                    fe = normed[:, 0, 2:2 + SEQ]
                    dve.wait_ge(proj_free[1], FREE1_IN1 + h + 1)
                    if h:
                        dve.wait_ge(lk_done, 8 * h)
                        dve.wait_ge(lev_full, h)
                    link(nc.vector.tensor_scalar(fe, fe, 1.0, None, ALU.add))
                    link(nc.vector.reciprocal(fe, fe))
                    link(nc.vector.tensor_scalar(k_hg[:], fe, lower[:, 2, h:h + 1], None, ALU.mult))
                    link(nc.vector.tensor_scalar(fe, k_hg[:], -1.0, 1.0, ALU.mult, ALU.add))
                    nc.vector.tensor_scalar(fe, fe, TINY, None, ALU.max).then_inc(f_ready, 1)
                    dve.wait_ge(logf_done, h + 1)
                    if h:
                        dve.wait_ge(dec_done, h)
                    nc.vector.tensor_tensor_scan(cum[:], starts[:], fe, 0.0, ALU.mult, ALU.add
                                                 ).then_inc(cum_done, 1)
                    dve.wait_ge(cum_done, h + 1)
                    for j in range(LEVELS + 1):
                        if j == LEVELS:
                            v = cum[:].rearrange("p (t n) -> p t n", n=P)
                            nc.vector.tensor_tensor(
                                level_e[:, j, :].rearrange("p (t n) -> p t n", n=P),
                                v[:, :, P - 1:P].to_broadcast([P, TB, P]), v, ALU.subtract).then_inc(diff_done, 1)
                            break
                        half = 1 << j
                        v = cum[:].rearrange("p (b two r) -> p b two r", two=2, r=half)
                        e = level_e[:, j, :].rearrange("p (b two r) -> p b two r", two=2, r=half)
                        mid = v[:, :, 0, half - 1:half].to_broadcast([P, SEQ // (2 * half), half])
                        nc.vector.tensor_tensor(e[:, :, 0, :], mid, v[:, :, 0, :], ALU.subtract)
                        last = nc.vector.tensor_tensor(e[:, :, 1, :], v[:, :, 1, :], mid, ALU.subtract)
                        if j == 3:
                            last.then_inc(diff_done, 1)
                    split(u + 4, 0)
                    dve.wait_ge(proj_free[0], FREE0_IN1 + 2 * h + 2)
                    dve.wait_ge(dec_done, h + 1)
                    nc.vector.tensor_tensor(q_dec[:, h % 2, :], q_hg[:], decay[:], ALU.mult)
                    nc.vector.tensor_copy(last_dec[:, h % 2, :],
                                          decay[:].rearrange("p (t n) -> p t n", n=P)[:, :, P - 1])
                    for j in range(LEVELS):
                        half = 1 << j
                        dve.wait_ge(level_exp, 2 * h + 1 + j // 4)
                        e = level_e[:, j, :].rearrange("p (b two r) -> p b two r", two=2, r=half)[:, :, 1, :]
                        qv = q_hg[:].rearrange("p (b two r) -> p b two r", two=2, r=half)[:, :, 1, :]
                        last = nc.vector.tensor_tensor(
                            level_q[:, j, :].rearrange("p (b r) -> p b r", r=half), e, qv, ALU.mult)
                    last.then_inc(lq_done, 1)
                    split(u + 5, 1)
                    ge = normed[:, 1, 2:2 + SEQ]
                    dve.wait_ge(gexp_done, h + 1)
                    link(nc.vector.tensor_scalar(ge, ge, 1.0, None, ALU.add))
                    link(nc.vector.reciprocal(ge, ge))
                    nc.vector.tensor_tensor(gate_o[:, h % 2, :], proj[1][:], ge, ALU.mult).then_inc(g_done, 1)
                if h:
                    dve.wait_ge(orstd_done, p + 1)
                    nc.vector.tensor_tensor(square[:, 1, :], obank[:], square[:, 1, :], ALU.mult
                                            ).then_inc(ho_free, 1)
                    dve.wait_ge(ho_free, p + 1)
                    nc.vector.scalar_tensor_tensor(out=oT1[:, p, :], in0=square[:, 1, :], scalar=onorm,
                                                   in1=gate_o[:, p % 2, :], op0=ALU.mult, op1=ALU.mult
                                                   ).then_inc(ho_done, 1)
                u += 4
            for dc in range(DC):
                low(h_base["o1"], dc, oT1[:, dc, :])
            mod_group(10)
            mod_group(11)
            out_units(U_OUT1, 3, 8)
            ffn(1, U_FFN1, FB)
            down(U_DOWN1, 4, 11, last=True)

            dve.wait_ge(rstd_done, 5)
            for dc in range(DC + 1):
                if dc < DC:
                    if dc >= 2:
                        dve.wait_ge(fin_y, dc - 1)
                    nc.vector.tensor_tensor(normed[:, dc % 2, 2:2 + SEQ], xT[:, dc, :], rstd[:], ALU.mult
                                            ).then_inc(fin_mul, 1)
                if dc:
                    dve.wait_ge(fin_full, dc)
                    nc.vector.tensor_copy(out_nat[:, :, (dc - 1) * P:dc * P],
                                          zb[(dc - 1) % 4][:].rearrange("p (t n) -> p t n", t=TB)
                                          ).then_inc(fin_evac, 1)

        @block.tensor
        def _(pe):
            def mm(dst, weights_ap, moving, start=False, stop=False):
                return nc.tensor.matmul(dst, weights_ap, moving, start=start, stop=stop,
                                        skip_group_check=True)

            def misc_wait(name):
                if MISC_AT[name]:
                    pe.wait_ge(misc_free, MISC_AT[name])

            def parts_ready(u):
                pe.wait_ge(hi_done, u + 1)
                pe.wait_ge(lo_done, u + 1)

            def unit(u, slot, dst, h_from=None):
                parts_ready(u)
                for k in range(DC):
                    if h_from is not None:
                        pe.wait_ge(h_lo, h_from + k + 1)
                    at = slice(k * P, (k + 1) * P)
                    mm(dst, w_hi[:, slot, at], hT_hi[:, k, :], start=(k == 0))
                    mm(dst, w_hi[:, slot, at], hT_lo[:, k, :])
                    last = mm(dst, w_lo[:, slot, at], hT_hi[:, k, :], stop=(k == DC - 1))
                last.then_inc(unit_mm, 1)

            def norm_sum(n):
                pe.wait_ge(ss_done, 7 * n + 7)
                misc_wait(f"norm{n}")
                mm(misc[:], ones, sumsq[:], True, True).then_inc(misc_full, 1)

            def mod_sum(g):
                if g < 2:
                    pe.wait_ge(ada_used, DC * (g + 1))
                else:
                    pe.wait_ge(sum_pool, (DC - 1) * (g - 1))
                misc_wait(f"mod{g}")
                for dc in range(DC):
                    last = mm(misc[:, dc:dc + 1], ada_sum[:, g % 4, dc * P:(dc + 1) * P], ones[:, 0:1],
                              True, True)
                last.then_inc(misc_full, 1)

            pe.wait_ge(const_in, 64)
            pe.wait_ge(small_in, 16 * 11)
            for i, n in enumerate((96, 96, 96, 96)):
                misc_wait(f"small{i}")
                nc.tensor.transpose(misc[:, 0:n], small_nat[0:n, i, :], ident[0:n, 0:n]).then_inc(misc_full, 1)
            pe.wait_ge(x_in, 16)
            for dc in range(DC):
                if dc >= 4:
                    pe.wait_ge(x_new, dc - 3)
                for t in range(TB):
                    last = nc.tensor.transpose(zb[dc % 4][:, t * P:(t + 1) * P],
                                               x_nat[:, t, dc * P:(dc + 1) * P], ident)
                last.then_inc(xt_full, 1)
            norm_sum(0)
            mod_sum(0)
            mod_sum(1)

            def tile_in(b):
                n = UNITS0.index(b)
                pe.wait_ge(proj_free[n % 2], n // 2 + 1)

            pe.wait_ge(tables_ready, SW_HEADS)
            u = 0
            for kind, b in STEPS0:
                if kind == "u":
                    if u >= 2:
                        pe.wait_ge(proj_free[u % 2], u // 2)
                    unit(u, u % 2, proj[u % 2][:], 0 if u == 0 else None)
                    u += 1
                elif kind == "T":
                    tile_in(SV + b)if b < 4 else tile_in(WV)
                    misc_wait(f"V{b}")
                    for t in range(TB):
                        last = nc.tensor.transpose(misc[:, t * P:(t + 1) * P],
                                                   vT0[:, b % 2, t * P:(t + 1) * P], ident)
                    last.then_inc(misc_full, 1)
                elif kind == "A":
                    hp, r = b // 2, slice(HEAD * (b % 2), HEAD * (b % 2) + HEAD)
                    tile_in(SQ + hp)
                    tile_in(SK + hp)
                    for j in range(TB):
                        if b:
                            pe.wait_ge(wt_done, 4 * (b - 1) + j + 1)
                        mm(zb[j][:, 0:Z_LEN[j]], k_sb[r, hp, j * P:(j + 1) * P], q_sb[r, hp, j * P:SEQ],
                           start=True)
                        mm(zb[j][:, 0:P], ident_r[:], strict_r[:], stop=True).then_inc(z_full, 1)
                elif kind == "B":
                    pe.wait_ge(sp_done, 4 * b + 4)
                    for j in range(TB):
                        own = softplus[:, b % 2, Z_OFF[j]:Z_OFF[j] + Z_LEN[j]]
                        last = mm(zb[j][:, 0:Z_LEN[j]], suffix, own, stop=(j == TB - 1))
                        for j2 in range(j + 1, TB):
                            last = mm(zb[j][:, (j2 - j) * P:Z_LEN[j]], minus,
                                      softplus[:, b % 2, Z_OFF[j2]:Z_OFF[j2] + Z_LEN[j2]],
                                      stop=(j2 == TB - 1))
                        last.then_inc(cum_full, 1)
                else:
                    hp, r = b // 2, slice(HEAD * (b % 2), HEAD * (b % 2) + HEAD)
                    pe.wait_ge(wt_done, 4 * b + 4)
                    pe.wait_ge(misc_free, MISC_AT[f"V{hp}"] + 1)
                    if b % 2 == 0 and hp:
                        pe.wait_ge(o_free, hp)
                    for j in range(TB):
                        last = mm(obank[r, j * P:SEQ], v_nat0[:, j, hp * P + r.start:hp * P + r.stop],
                                  weights[:, Z_OFF[j]:Z_OFF[j] + Z_LEN[j]], start=(j == 0), stop=(j == TB - 1))
                    last.then_inc(pv_done, 1)

            def window_logits(h):
                s, hp, g = h % 2, h // 2, h // SW_GROUP
                r = slice(HEAD * s, HEAD * s + HEAD)
                tile_in(WQ + hp)
                if h >= 2:
                    pe.wait_ge(pt_act, h - 1)
                    pe.wait_ge(pt_dve, h - 1)
                mm(zb[2 * s][:, 0:3 * P], slope_r[:, h, :], band_r[:, P:4 * P], start=True)
                for b in range(TB):
                    z, lo, _, n = window_block(b, s)
                    if b == 2:
                        mm(z[:], slope_r[:, h, :], band_r[:], start=True)
                    last = mm(z[:, lo:lo + n], q_sw[r, hp, b * P:(b + 1) * P],
                              k_sw[r, g, (b + 1) * P - n:(b + 1) * P], stop=True)
                    if b % 2:
                        last.then_inc(sw_full, 1)

            def window_transposes(h):
                pe.wait_ge(p_norm, 4 * h + 4)
                p_buf = (soft_a, weights)[h % 2]
                for i in range(7):
                    z, at = (zb[2 * (h % 2)], i) if i < 3 else (zb[2 * (h % 2) + 1], i - 3)
                    last = nc.tensor.transpose(z[:, at * P:(at + 1) * P], p_buf[:, i * P:(i + 1) * P], ident)
                    if i in (2, 6):
                        last.then_inc(pt_full, 1)

            def window_values(h):
                s, g = h % 2, h // SW_GROUP
                r = slice(HEAD * s, HEAD * s + HEAD)
                v_at = slice(4 * P + HEAD * g, 4 * P + HEAD * g + HEAD)
                pe.wait_ge(pt_act, h + 1)
                pe.wait_ge(pt_dve, h + 1)
                if s == 0:
                    pe.wait_ge(o_free, 4 + h // 2)
                for b in range(TB):
                    _, _, at, n = window_block(b, s)
                    blocks = [b] if b == 0 else [b - 1, b]
                    for i, kb in enumerate(blocks):
                        last = mm(obank[r, b * P:(b + 1) * P], v_nat0[:, kb, v_at],
                                  softplus[:, s, at + i * P:at + (i + 1) * P], start=(b == 0), stop=(kb == b))
                last.then_inc(pv_done, 1)

            window_logits(0)
            for h in range(SW_HEADS):
                if h + 1 < SW_HEADS:
                    window_logits(h + 1)
                window_transposes(h)
                window_values(h)

            def out_units(u0, n, base):
                for o in range(DC):
                    if o == 0 and n == 1:
                        mod_sum(2)
                    if o >= 2:
                        pe.wait_ge(x_new, 8 * n + o - 1)
                    elif n == 1:
                        pe.wait_ge(proj_free[o], FREE_OUT0)
                    else:
                        pe.wait_ge((proj_free[0], g_done)[o], (FREE0_FFN[1], HG_HEADS)[o])
                    unit(u0 + o, o % 2, proj[o % 2][:], base if o == 0 else None)
                if n == 1:
                    for g in (3, 4, 5):
                        mod_sum(g)
                norm_sum(n)

            def ffn(layer, u0, base, h_from):
                with pe.Fori(0, FB) as f:
                    pe.wait_ge(proj_free[0], FREE0_FFN[layer] + f)
                    unit(u0 + 2 * f, 0, proj[0][:], h_from)
                    pe.wait_ge(gp_done, base + f + 1)
                    unit(u0 + 2 * f + 1, 1, proj[1][:])

            def down(layer, u0, n):
                def one(u, slot, block, first=False, last_one=False):
                    parts_ready(u)
                    for k in range(2):
                        hi = gated_hi[layer][:, bass.ds(block + k, 1), :].rearrange("p a n -> p (a n)")
                        lo = gated_lo[layer][:, bass.ds(block + k, 1), :].rearrange("p a n -> p (a n)")
                        for q in range(4):
                            at = slice(k * 512 + q * P, k * 512 + (q + 1) * P)
                            if first and k == 0 and u > u0:
                                pe.wait_ge(x_new, 8 * n + q + 1)
                            mm(zb[q][:], w_hi[:, slot, at], hi, start=first and k == 0)
                            mm(zb[q][:], w_hi[:, slot, at], lo)
                            last = mm(zb[q][:], w_lo[:, slot, at], hi, stop=last_one and k == 1)
                    last.then_inc(unit_mm, 1)

                pe.wait_ge(gp_lo, FB * (layer + 1))
                one(u0, 0, 0, first=True)
                one(u0 + 1, 1, 2)
                with pe.Fori(1, HALF // 2) as i:
                    for s in range(2):
                        one(u0 + 2 * i + s, s, 4 * i + 2 * s)
                one(u0 + HALF - 1, 0, FB - 2, last_one=True)
                one(u0 + HALF, 1, 0, first=True)
                with pe.Fori(0, HALF // 2 - 1) as i:
                    for s in range(2):
                        one(u0 + HALF + 1 + 2 * i + s, s, 4 * i + 2 * s + 2)
                one(u0 + FB - 2, 0, FB - 4)
                one(u0 + FB - 1, 1, FB - 2, last_one=True)
                norm_sum(n)

            out_units(U_OUT0, 1, h_base["o0"])
            ffn(0, U_FFN0, 0, h_base["norm1"])
            for g in range(6, 10):
                mod_sum(g)
            down(0, U_DOWN0, 2)

            u = U_IN1
            for h in range(HG_HEADS + 1):
                p = h - 1
                if h < HG_HEADS:
                    pe.wait_ge(proj_free[0], FREE0_IN1 + 2 * h)
                    unit(u, 0, proj[0][:], h_base["norm2"] if h == 0 else None)
                if h:
                    pe.wait_ge(proj_free[0], FREE0_IN1 + 2 * p + 1)
                    misc_wait(f"val{p}")
                    for t in range(TB):
                        last = nc.tensor.transpose(misc[:, t * P:(t + 1) * P], vT1[:, t * P:(t + 1) * P], ident)
                    last.then_inc(misc_full, 1)
                    pe.wait_ge(lk_done, (LEVELS + 1) * p + 1)
                    misc_wait(f"key{p}")
                    for t in range(TB - 1):
                        last = nc.tensor.transpose(misc[:, t * P:(t + 1) * P],
                                                   level_k[:, LEVELS, t * P:(t + 1) * P], ident)
                    last.then_inc(misc_full, 1)
                if h < HG_HEADS:
                    if h:
                        pe.wait_ge(g_done, h)
                    else:
                        pe.wait_ge(proj_free[1], FREE1_IN1)
                    unit(u + 1, 1, proj[1][:])
                if h:
                    pe.wait_ge(lk_done, (LEVELS + 1) * (p + 1))
                    pe.wait_ge(lq_done, p + 1)
                    if p:
                        pe.wait_ge(score_done, LEVELS * p)
                    misc_wait(f"diag{p}")
                    for t in range(TB):
                        at = slice(t * P, (t + 1) * P)
                        last = mm(misc[:, at], k_hg[:, at], q_hg[:, at], True, True)
                    last.then_inc(misc_full, 1)
                    for j in range(LEVELS):
                        for t in range(TB):
                            lo = 256 * (j % 2) + 64 * t
                            last = mm(zb[j // 2][:, lo:lo + 64], level_k[:, j, t * P:(t + 1) * P],
                                      level_q[:, j, 64 * t:64 * t + 64], True, True)
                    last.then_inc(lev_full, 1)
                    misc_wait(f"kv{p}")
                    for t in range(TB - 1):
                        last = mm(misc[:, t * P:(t + 1) * P], key_nat[:, t, :], v_nat1[:, t, :], True, True)
                    last.then_inc(misc_full, 1)
                if h < HG_HEADS:
                    pe.wait_ge(proj_free[0], FREE0_IN1 + 2 * h + 1)
                    unit(u + 2, 0, proj[0][:])
                if h:
                    pe.wait_ge(score_done, LEVELS * (p + 1))
                    pe.wait_ge(misc_free, MISC_AT[f"kv{p}"] + 1)
                    if p:
                        pe.wait_ge(ho_free, p)
                    for t in range(TB):
                        at = slice(t * P, (t + 1) * P)
                        last = mm(obank[:, at], v_nat1[:, t, :], scores[:, at], start=(t == 0), stop=(t == 0))
                        if t:
                            last = mm(obank[:, at], states[:, t - 1, :], q_dec[:, p % 2, at], stop=True)
                    last.then_inc(ho_full, 1)
                if h < HG_HEADS:
                    pe.wait_ge(proj_free[1], FREE1_IN1 + h + 1)
                    unit(u + 3, 1, proj[1][:])
                if h:
                    pe.wait_ge(osq_done, p + 1)
                    misc_wait(f"osq{p}")
                    mm(misc[:], ones, square[:, 0, :], True, True).then_inc(misc_full, 1)
                u += 4
            mod_sum(10)
            mod_sum(11)
            out_units(U_OUT1, 3, h_base["o1"])
            ffn(1, U_FFN1, FB, h_base["norm3"])
            down(1, U_DOWN1, 4)

            for dc in range(DC):
                pe.wait_ge(fin_y, dc + 1)
                if dc >= 4:
                    pe.wait_ge(fin_evac, dc - 3)
                for t in range(TB):
                    last = nc.tensor.transpose(zb[dc % 4][:, t * P:(t + 1) * P],
                                               h32[:, dc % 2, t * P:(t + 1) * P], ident)
                last.then_inc(fin_full, 1)


_INS = ["x", "c", "ada_w", "ada_b", "norm_mix_g", "norm_ffn_g", "ab_w_in", "ab_sinks", "ab_w_out",
        "hg_w_in", "hg_lb_gamma", "hg_onorm_g", "hg_w_out", "ffn_w_gate", "ffn_w_up", "ffn_conv_w",
        "ffn_conv_b", "ffn_w_down", "final_g"]


def kernel(**inputs):
    import concourse.bacc as bacc
    from concourse.bass_utils import run_bass_kernel_spmd

    nc = bacc.Bacc("TRN2", target_bir_lowering=False, num_devices=1)
    arrays = {name: np.ascontiguousarray(inputs[name]) for name in _INS}
    arrays["tables"], levels = constant_tables()
    arrays["level_masks"] = levels.reshape(P, -1)
    args = [nc.dram_tensor(name, a.shape, mybir.dt.from_np(a.dtype), kind="ExternalInput").ap()
            for name, a in arrays.items()]
    result = nc.dram_tensor("result", (1, SEQ, D), F32, kind="ExternalOutput").ap()
    trunk(nc, *args, result)
    r = run_bass_kernel_spmd(nc, [arrays], core_ids=[0])
    return r.results[0]["result"]
```

```python
from contextlib import ExitStack

import concourse.bass as bass
import numpy as np
from concourse import mybir

F32 = mybir.dt.float32
F32R = mybir.dt.float32r
U32 = mybir.dt.uint32
ALU = mybir.AluOpType
ACT = mybir.ActivationFunctionType
AX = mybir.AxisListType

P = 128
SEQ = 512
D = 1024
DC = D // P
TB = SEQ // P
DEPTH = 2
HEAD = 64
SB_HEADS = 8
SW_HEADS = 8
SW_GROUP = 4
CHUNK = 64
HG_HEADS = 8
D_FF = 2816
FB = D_FF // P
EPS = 1e-6
NEG = -1e30
LEVELS = 7
POOL_LEVELS = (0, 1, 2, 3, LEVELS, 4, 5, 6)
BELOW_ONE = 1.0 - 2.0 ** -24
CLAMP = 40.0
EXP_LN_SET = "natural_log_exp_and_others"
GELU_SET = "gelu_apprx_tanh_and_others"
MODS = 6
UNIT = 1024

SQ, SK, SV, WQ, WK, WV = 0, 4, 8, 12, 16, 17

STEPS0 = [
    ("u", SQ), ("u", SK), ("u", SV), ("A", 0), ("u", WK), ("T", 0), ("B", 0), ("u", WV), ("C", 0),
    ("A", 1), ("u", SQ + 1), ("T", 4), ("B", 1), ("u", SK + 1), ("C", 1),
    ("u", SV + 1), ("A", 2), ("u", WQ), ("T", 1), ("B", 2), ("u", WQ + 1), ("C", 2),
    ("A", 3), ("u", SQ + 2), ("B", 3), ("u", SK + 2), ("C", 3),
    ("u", SV + 2), ("A", 4), ("u", WQ + 2), ("T", 2), ("B", 4), ("u", SQ + 3), ("C", 4),
    ("A", 5), ("u", SK + 3), ("B", 5), ("u", SV + 3), ("C", 5),
    ("A", 6), ("u", WQ + 3), ("T", 3), ("B", 6), ("C", 6), ("A", 7), ("B", 7), ("C", 7),
]
UNITS0 = [b for kind, b in STEPS0 if kind == "u"]

U_IN0 = 0
U_OUT0 = U_IN0 + len(UNITS0)
U_FFN0 = U_OUT0 + DC
U_DOWN0 = U_FFN0 + 2 * FB
U_IN1 = U_DOWN0 + FB
U_OUT1 = U_IN1 + 4 * HG_HEADS
U_FFN1 = U_OUT1 + DC
U_DOWN1 = U_FFN1 + 2 * FB
U_END = U_DOWN1 + FB
HALF = FB // 2

MISC = (
    [f"small{i}" for i in range(4)]
    + ["norm0", "mod0", "mod1"]
    + [f"V{b}" for kind, b in STEPS0 if kind == "T"]
    + ["mod2", "mod3", "mod4", "mod5", "norm1", "mod6", "mod7", "norm2"]
    + [name for h in range(HG_HEADS + 2)
       for name in ([f"osq{h - 2}"] if h > 1 else [])
       + ([f"{what}{h - 1}" for what in ("val", "key", "diag", "kv")] if 0 < h <= HG_HEADS else [])
       + ([f"mod{7 + h}"] if 1 <= h <= 4 else [])]
    + ["norm3", "norm4"]
)
MISC_AT = {name: i for i, name in enumerate(MISC)}

FREE_OUT0 = len(UNITS0) // 2
FREE0_FFN = [FREE_OUT0, FREE_OUT0 + FB + 2 * HG_HEADS]
FREE0_IN1 = FREE_OUT0 + FB

Z_OFF = [0, 512, 896, 1152]
Z_LEN = [SEQ - P * j for j in range(TB)]
Z_ALL = sum(Z_LEN)


def constant_tables():
    s = np.arange(P)[:, None]
    q = np.arange(P)[None, :]
    ident = np.eye(P)
    ones = np.ones((P, P))
    suffix = np.where(s >= q, -1.0, 0.0)
    strict = np.where(s < q, 0.0, NEG)
    bands = []
    for first in (-P, 0):
        gap = s // CHUNK - (q + first) // CHUNK
        bands.append(np.where((gap >= 0) & (gap < 2), -np.abs(s - (q + first)), NEG))
    tables = np.concatenate([ident, ones, suffix, -ones, strict] + bands * 2, axis=1)
    levels = np.zeros((P, LEVELS, 2 * P))
    n = np.arange(2 * P) % 64
    for j in range(LEVELS):
        half = 1 << j
        start = (n // half) * 2 * half
        levels[:, j, :] = (s >= start) & (s < start + half)
    return tables.astype(np.float32), levels.astype(np.float32)


def trunk(nc, x, c, ada_w, ada_b, norm_mix_g, norm_ffn_g, ab_w_in, ab_sinks, ab_w_out, hg_w_in,
          hg_lb_gamma, hg_onorm_g, hg_w_out, ffn_w_gate, ffn_w_up, ffn_conv_w, ffn_conv_b,
          ffn_w_down, final_g, tables, level_masks, out):
    with ExitStack() as ctx:
        def sem(name):
            return ctx.enter_context(nc.semaphore(name))

        def sb(name, shape, dt=F32, scope=ctx):
            return scope.enter_context(nc.sbuf_tensor(name, shape, dt))

        def bank(name):
            return ctx.enter_context(nc.psum_tensor(name, [P, 512], F32))

        xT = sb("xT", [P, DC, SEQ])
        hT_hi = sb("hT_hi", [P, DC, SEQ], F32R)
        hT_lo = sb("hT_lo", [P, DC, SEQ], F32R)
        w_raw = sb("w_raw", [P, 2, UNIT])
        w_hi = sb("w_hi", [P, 2, UNIT], F32R)
        w_lo = sb("w_lo", [P, 2, UNIT], F32R)
        ada_raw = sb("ada_raw", [P, 2, UNIT])
        ada_part = sb("ada_part", [P, UNIT])
        ada_sum = sb("ada_sum", [P, 4, UNIT])
        normed = sb("normed", [P, 2, SEQ + 2])
        h32 = sb("h32", [P, 2, SEQ])
        square = sb("square", [P, 2, SEQ])
        sumsq = sb("sumsq", [P, SEQ])
        rstd = sb("rstd", [P, SEQ])
        table = sb("table", [P, 2 * P])
        ident, ones = table[:, 0:P], table[:, P:2 * P]
        small = sb("small", [P, 4, 96])
        mod = sb("mod", [P, DEPTH * MODS, DC])
        scale_g = sb("scale_g", [P, 4, DC])
        cond = sb("cond", [P, 3, DC])
        lower = sb("lower", [P, 3, DC])

        table2 = h32[:].rearrange("p a n -> p (a n)")[:, 0:7 * P]
        small_nat = rstd[:].rearrange("p (a n) -> p a n", a=4)

        with ExitStack() as s0:
            ident_r = sb("ident_r", [P, P], F32R, s0)
            table_r = sb("table_r", [P, 7 * P], F32R, s0)
            suffix, minus, strict_r = [table_r[:, i * P:(i + 1) * P] for i in range(3)]
            band_r = table_r[:, 3 * P:7 * P]
            slope_r = sb("slope_r", [P, SW_HEADS, P], F32R, s0)
            sinks = sb("sinks", [P, SW_HEADS], F32, s0)
            soft = sb("soft", [P, 3, 4, TB], F32, s0)
            with ExitStack() as start:
                x_nat = sb("x_nat", [P, TB, D], F32, start)
                ada_first = sb("ada_first", [P, 4, 4, UNIT], F32, start)
            q_sb = sb("q_sb", [P, 4, SEQ], F32, s0)
            k_sb = sb("k_sb", [P, 4, SEQ], F32, s0)
            q_sw = sb("q_sw", [P, 4, SEQ], F32, s0)
            k_sw = sb("k_sw", [P, 2, SEQ], F32, s0)
            vT0 = sb("vT0", [P, 2, SEQ], F32, s0)
            v_nat0 = sb("v_nat0", [P, TB, 5 * P], F32, s0)
            soft_a = sb("soft_a", [P, Z_ALL], F32, s0)
            weights = sb("weights", [P, Z_ALL], F32, s0)
            with ExitStack() as window:
                pt_pair = sb("pt_pair", [P, 2, Z_ALL], F32, window)
            softplus = sb("softplus", [P, 2, Z_ALL], F32R, s0)
            oT0 = sb("oT0", [P, DC, SEQ], F32, s0)
        with ExitStack() as s1:
            vT1 = sb("vT1", [P, SEQ], F32, s1)
            v_nat1 = sb("v_nat1", [P, TB, P], F32, s1)
            k_hg = sb("k_hg", [P, SEQ], F32, s1)
            q_hg = sb("q_hg", [P, SEQ], F32, s1)
            cum = sb("cum", [P, SEQ], F32, s1)
            decay = sb("decay", [P, SEQ], F32, s1)
            level_e = sb("level_e", [P, LEVELS + 1, SEQ], F32, s1)
            level_k = sb("level_k", [P, LEVELS + 1, SEQ], F32, s1)
            level_q = sb("level_q", [P, LEVELS, 2 * P], F32, s1)
            q_dec = sb("q_dec", [P, 2, SEQ], F32, s1)
            gate_o = sb("gate_o", [P, 2, SEQ], F32, s1)
            scores = sb("scores", [P, SEQ], F32, s1)
            states = sb("states", [P, 3, P], F32, s1)
            key_nat = sb("key_nat", [P, 3, P], F32, s1)
            last_dec = sb("last_dec", [P, 2, TB], F32, s1)
            masks = sb("masks", [P, LEVELS, 2 * P], F32, s1)
            oT1 = sb("oT1", [P, DC, SEQ], F32, s1)
        starts = rstd
        gated_hi, gated_lo = [], []
        for layer in range(DEPTH):
            with ExitStack() as sf:
                gated_hi.append(sb(f"gated_hi{layer}", [P, FB, SEQ], F32R, sf))
                gated_lo.append(sb(f"gated_lo{layer}", [P, FB, SEQ], F32R, sf))
        with ExitStack() as send:
            out_nat = sb("out_nat", [P, TB, D], F32, send)

        proj = [bank("proj0"), bank("proj1")]
        zb = [bank(f"z{j}") for j in range(4)]
        obank = bank("obank")
        misc = bank("misc")
        pairs = [(zb[0], zb[1]), (zb[2], zb[3]), (proj[0], proj[1])]
        p_bufs = [soft_a, weights, q_sb[:].rearrange("p a n -> p (a n)")]
        pt_bufs = [pt_pair[:, 0, :], pt_pair[:, 1, :], k_sb[:].rearrange("p a n -> p (a n)")]

        const_in = sem("const_in")
        small_in = sem("small_in")
        x_in = sem("x_in")
        masks_in = sem("masks_in")
        raw_in = [sem("raw_in0"), sem("raw_in1")]
        ada_in = [sem("ada_in0"), sem("ada_in1")]
        ada_first_in = [sem(f"ada_first_in{i}") for i in range(4)]
        out_done = sem("out_done")
        hi_done = sem("hi_done")
        lo_done = sem("lo_done")
        unit_mm = sem("unit_mm")
        proj_free = [sem("proj_free0"), sem("proj_free1")]
        misc_full = sem("misc_full")
        misc_free = sem("misc_free")
        small_clear = sem("small_clear")
        act_chain = sem("act_chain")
        dve_chain = sem("dve_chain")
        pool_chain = sem("pool_chain")
        tables_ready = sem("tables_ready")
        small_ready = sem("small_ready")
        cond_exp = sem("cond_exp")
        cond_ready = sem("cond_ready")
        ada_used = sem("ada_used")
        sum_dve = sem("sum_dve")
        sum_pool = sem("sum_pool")
        mod_ready = sem("mod_ready")
        xt_full = sem("xt_full")
        x_new = sem("x_new")
        sq_done = sem("sq_done")
        ss_done = sem("ss_done")
        rstd_done = sem("rstd_done")
        normed_done = sem("normed_done")
        h_hi = sem("h_hi")
        h_lo = sem("h_lo")
        tile_ready = sem("tile_ready")
        tile_dve = sem("tile_dve")
        v_ready = sem("v_ready")
        z_full = sem("z_full")
        abs_done = sem("abs_done")
        log_done = sem("log_done")
        sp_sum = sem("sp_sum")
        sp_hi = sem("sp_hi")
        sp_done = sem("sp_done")
        cum_full = sem("cum_full")
        wt_done = sem("wt_done")
        pv_done = sem("pv_done")
        o_free = sem("o_free")
        sw_full = sem("sw_full")
        max_done = sem("max_done")
        p_done = sem("p_done")
        p_norm = sem("p_norm")
        pt_full = sem("pt_full")
        pt_act = sem("pt_act")
        pt_dve = sem("pt_dve")
        hv_ready = sem("hv_ready")
        hvn_ready = sem("hvn_ready")
        fexp_done = sem("fexp_done")
        f_ready = sem("f_ready")
        logf_done = sem("logf_done")
        cum_done = sem("cum_done")
        diff_dve = sem("diff_dve")
        diff_pool = sem("diff_pool")
        f_clamped = sem("f_clamped")
        g_clamped = sem("g_clamped")
        dec_done = sem("dec_done")
        level_exp = sem("level_exp")
        lk_done = sem("lk_done")
        hq_ready = sem("hq_ready")
        lq_done = sem("lq_done")
        keyn_ready = sem("keyn_ready")
        lev_full = sem("lev_full")
        score_done = sem("score_done")
        state_done = sem("state_done")
        gexp_done = sem("gexp_done")
        g_done = sem("g_done")
        ho_full = sem("ho_full")
        osq_done = sem("osq_done")
        orstd_done = sem("orstd_done")
        ho_free = sem("ho_free")
        ho_done = sem("ho_done")
        ga_done = sem("ga_done")
        conv_done = sem("conv_done")
        gelu_done = sem("gelu_done")
        gp_done = sem("gp_done")
        gp_hi = sem("gp_hi")
        gp_lo = sem("gp_lo")
        down_full = sem("down_full")
        fin_y = sem("fin_y")
        fin_full = sem("fin_full")
        fin_evac = sem("fin_evac")

        bias_col = small[:, 0, 0:96]
        c_col = small[:, 1, 0:8]
        mix_g = [small[:, 1, 8 + 8 * i:16 + 8 * i] for i in range(2)]
        ffn_g = [small[:, 1, 24 + 8 * i:32 + 8 * i] for i in range(2)]
        fin_g = small[:, 1, 40:48]
        gamma = [small[:, 1, 48 + 8 * i:56 + 8 * i] for i in range(2)]
        onorm = small[:, 1, 64:65]
        norm_g = [mix_g[0], ffn_g[0], mix_g[1], ffn_g[1]]

        def conv_col(layer, tap, f):
            return small[:, 2 + layer, bass.ds(f + tap * FB, 1)]

        h_base = {"norm0": 0, "o0": 8, "norm1": 16, "norm2": 24, "o1": 32, "norm3": 40}

        def window_block(b, s):
            z = pairs[s][b // 2]
            lo, n = ((0, P), (P, 2 * P), (0, 2 * P), (2 * P, 2 * P))[b]
            at = (0, P, 3 * P, 5 * P)[b]
            return z, lo, at, n

        def level_views(j):
            half = 1 << j
            v = cum[:].rearrange("p (b two r) -> p b two r", two=2, r=half)
            e = level_e[:, j, :].rearrange("p (b two r) -> p b two r", two=2, r=half)
            mid = v[:, :, 0, half - 1:half].to_broadcast([P, SEQ // (2 * half), half])
            return v[:, :, 0, :], v[:, :, 1, :], mid, e[:, :, 0, :], e[:, :, 1, :]

        block = ctx.enter_context(nc.Block())

        @block.sync
        def _(sp):
            def slot_free(u):
                sp.wait_ge(lo_done, u - 1)

            def load(slot, dst_shape, src):
                a, b = dst_shape
                sp.dma_start(w_raw[:, slot, :].rearrange("p (a b) -> p a b", a=a, b=b),
                             src).then_inc(raw_in[slot], 16)

            def columns(w, at, n=P):
                return w[:, bass.ds(at, n)].rearrange("(k p) n -> p k n", p=P)

            def rows(dst, lo, n, src):
                sp.dma_start(small_nat[lo:lo + n, dst, :], src).then_inc(small_in, 16)

            sp.dma_start(x_nat[:], x[0].rearrange("(t p) d -> p t d", p=P)).then_inc(x_in, 16)
            sp.wait_ge(small_clear, 1)
            rows(1, 0, 8, c.rearrange("b (r p) -> (b r) p", p=P))
            rows(1, 48, 16, hg_lb_gamma.rearrange("l (r p) -> (l r) p", p=P))
            sp.dma_start(table[:], tables[:, 0:2 * P]).then_inc(const_in, 16)
            rows(0, 0, 96, ada_b.rearrange("l (r p) -> (l r) p", p=P))
            rows(1, 8, 16, norm_mix_g.rearrange("l (r p) -> (l r) p", p=P))
            rows(1, 24, 16, norm_ffn_g.rearrange("l (r p) -> (l r) p", p=P))
            rows(1, 40, 8, final_g.rearrange("(r p) -> r p", p=P))
            rows(1, 64, 1, hg_onorm_g)
            for layer in range(DEPTH):
                rows(2 + layer, 0, 3 * FB, ffn_conv_w[layer].rearrange("w (r p) -> (w r) p", p=P))
                rows(2 + layer, 3 * FB, FB, ffn_conv_b[layer].rearrange("(r p) -> r p", p=P))
            sp.dma_start(table2, tables[:, 2 * P:9 * P]).then_inc(const_in, 16)
            sp.dma_start(sinks[:], ab_sinks.partition_broadcast(P).rearrange("p a h -> p (a h)")
                         ).then_inc(const_in, 16)
            for i in range(4):
                g, k = i // 2, 4 * (i % 2)
                sp.dma_start(ada_first[:, i, :, :],
                             ada_w[0, k * P:(k + 4) * P, g * D:(g + 1) * D].rearrange("(k p) n -> p k n", p=P)
                             ).then_inc(ada_first_in[i], 16)

            for u, b in enumerate(UNITS0):
                if u >= 2:
                    slot_free(u)
                load(u % 2, (DC, P), columns(ab_w_in[0], P * b))

            def out_units(u0, w):
                with sp.Fori(0, DC // 2) as i:
                    for s in range(2):
                        slot_free(u0 + 2 * i + s)
                        load(s, (DC, P), columns(w, i * (2 * P) + P * s))

            def ffn_units(layer, u0):
                with sp.Fori(0, FB) as f:
                    for s, w in enumerate((ffn_w_gate[layer], ffn_w_up[layer])):
                        slot_free(u0 + 2 * f + s)
                        load(s, (DC, P), columns(w, f * P))

            def down_units(layer, u0):
                w = ffn_w_down[layer]

                def one(n, half, slot, u):
                    slot_free(u)
                    src = w[bass.ds(n * (2 * P), 2 * P), half * 512:half * 512 + 512]
                    load(slot, (2, 512), src.rearrange("(k p) n -> p k n", p=P))

                with sp.Fori(0, HALF // 2) as i:
                    for s in range(2):
                        one(2 * i + s, 0, s, u0 + 2 * i + s)
                one(HALF - 1, 0, 0, u0 + HALF - 1)
                one(0, 1, 1, u0 + HALF)
                with sp.Fori(0, HALF // 2) as i:
                    for s in range(2):
                        one(2 * i + (1 + s), 1, s, u0 + HALF + 1 + 2 * i + s)

            out_units(U_OUT0, ab_w_out[0])
            ffn_units(0, U_FFN0)
            down_units(0, U_DOWN0)
            for h in range(HG_HEADS):
                for n, part in enumerate((2, 1, 0, 3)):
                    slot_free(U_IN1 + 4 * h + n)
                    load(n % 2, (DC, P), columns(hg_w_in[0][:, part * D:(part + 1) * D], h * P))
            out_units(U_OUT1, hg_w_out[0])
            ffn_units(1, U_FFN1)
            down_units(1, U_DOWN1)

            out_view = out[0].rearrange("(t p) d -> p t d", p=P)
            for k in range(4):
                sp.wait_ge(fin_evac, 2 * k + 2)
                sp.dma_start(out_view[:, :, 2 * k * P:(2 * k + 2) * P],
                             out_nat[:, :, 2 * k * P:(2 * k + 2) * P]).then_inc(out_done, 16)
            sp.wait_ge(out_done, 64)

        @block.gpsimd
        def _(pool):
            def load(j):
                g, k = divmod(j, DC)
                layer, which = divmod(g, MODS)
                m = j - 2 * DC
                pool.dma_start(ada_raw[:, j % 2, :],
                               ada_w[layer, k * P:(k + 1) * P, which * D:(which + 1) * D]
                               ).then_inc(ada_in[m % 2], 16)

            chain = [0]
            total = DEPTH * MODS * DC
            pool.memset(small_nat, 0.0).then_inc(small_clear, 1)
            for j in range(2 * DC, 2 * DC + 2):
                load(j)
            for j in range(2 * DC, total):
                g, k = divmod(j, DC)
                if g >= 4 and k == 0:
                    pool.wait_ge(misc_full, MISC_AT[f"mod{g - 4}"] + 1)
                if k == 0 and g == 2:
                    pool.wait_ge(cond_ready, 1)
                pool.wait_ge(ada_in[j % 2], 16 * ((j - 2 * DC) // 2 + 1))
                acc = ada_sum[:, g % 4, :]
                scale = cond[:, 2, k:k + 1]
                if k == 0:
                    pool.tensor_scalar(acc, ada_raw[:, j % 2, :], scale, None, ALU.mult
                                       ).then_inc(pool_chain, 1)
                    chain[0] += 1
                    pool.wait_ge(pool_chain, chain[0])
                else:
                    pool.tensor_scalar(ada_part[:], ada_raw[:, j % 2, :], scale, None, ALU.mult
                                       ).then_inc(pool_chain, 1)
                    chain[0] += 1
                    pool.wait_ge(pool_chain, chain[0])
                    pool.tensor_tensor(acc, acc, ada_part[:], ALU.add).then_inc(sum_pool, 1)
                    pool.wait_ge(sum_pool, (g - 2) * (DC - 1) + k)
                if j + 2 < total:
                    load(j + 2)

            pool.wait_ge(x_new, 3 * DC)
            pool.dma_start(masks[:], level_masks.rearrange("p (j n) -> p j n", j=LEVELS)
                           ).then_inc(masks_in, 16)

            for h in range(HG_HEADS):
                pool.wait_ge(cum_done, h + 1)
                if h:
                    pool.wait_ge(lq_done, h)
                for j in range(4, LEVELS):
                    a, b, mid, to_mid, from_mid = level_views(j)
                    pool.tensor_tensor(to_mid, mid, a, ALU.subtract)
                    pool.tensor_tensor(from_mid, b, mid, ALU.subtract)
                v = cum[:].rearrange("p (t n) -> p t n", n=P)
                pool.tensor_tensor(level_e[:, LEVELS, :].rearrange("p (t n) -> p t n", n=P),
                                   v[:, :, P - 1:P].to_broadcast([P, TB, P]), v, ALU.subtract
                                   ).then_inc(diff_pool, 1)
                if h:
                    pool.wait_ge(lev_full, h)
                for j in POOL_LEVELS:
                    pool.wait_ge(level_exp, 2 * h + 1 + j // 4)
                    pool.tensor_tensor(level_k[:, j, :], level_e[:, j, :], k_hg[:], ALU.mult
                                       ).then_inc(lk_done, 1)

        @block.scalar
        def _(act):
            chain = [0]

            def link(ins):
                chain[0] += 1
                ins.then_inc(act_chain, 1)
                act.wait_ge(act_chain, chain[0])

            def split(u, slot):
                act.wait_ge(raw_in[slot], u * 8 + (16 - 8 * slot))
                if not (isinstance(u, int) and u < 2):
                    act.wait_ge(unit_mm, u - 1)
                nc.scalar.activation(w_hi[:, slot, :], w_raw[:, slot, :], ACT.Copy).then_inc(hi_done, 1)

            def squares(n, dc):
                act.wait_ge(x_new, 8 * n + dc + 1)
                if dc > 2:
                    act.wait_ge(ss_done, 6 * n + dc - 2)
                dst = square[:, dc % 2, :] if dc else sumsq[:]
                nc.scalar.activation(dst, xT[:, dc, :], ACT.Square).then_inc(sq_done, 1)

            def root(n):
                act.wait_ge(misc_full, MISC_AT[f"norm{n}"] + 1)
                nc.scalar.activation(rstd[:], misc[:], ACT.Ln, bias=EPS, scale=1.0 / D).then_inc(misc_free, 1)
                act.wait_ge(misc_free, MISC_AT[f"norm{n}"] + 1)
                nc.scalar.activation(rstd[:], rstd[:], ACT.Exp, scale=-0.5).then_inc(rstd_done, 1)

            def modulated(n):
                shift = mod[:, 6 * (n // 2) + 3 * (n % 2), :]
                for dc in range(DC):
                    act.wait_ge(normed_done, 8 * n + dc + 1)
                    nc.scalar.activation(hT_hi[:, dc, :], normed[:, dc % 2, 2:2 + SEQ], ACT.Identity,
                                         bias=shift[:, dc:dc + 1]).then_inc(h_hi, 1)

            def heads_hi(which, src, ready):
                for dc in range(DC):
                    ready(dc)
                    nc.scalar.activation(hT_hi[:, dc, :], src[:, dc, :], ACT.Copy).then_inc(h_hi, 1)

            act.preload_act_table_set(EXP_LN_SET)
            act.wait_ge(small_ready, 3)
            nc.scalar.activation(cond[:, 0, :], c_col, ACT.Exp, scale=-1.0)
            nc.scalar.activation(lower[:, 1, :], lower[:, 0, :], ACT.Exp).then_inc(cond_exp, 1)
            for dc in range(DC):
                squares(0, dc)
            split(0, 0)
            split(1, 1)
            root(0)
            modulated(0)

            u = 0
            n_act = [0]
            for kind, b in STEPS0:
                if kind == "u":
                    split(u + 2, u % 2)
                    if b < WQ:
                        act.wait_ge(unit_mm, u + 1)
                        if SV <= b:
                            if b - SV == 2:
                                act.wait_ge(misc_full, MISC_AT["V4"] + 1)
                            if b - SV == 3:
                                act.wait_ge(misc_full, MISC_AT["V1"] + 1)
                            nc.scalar.activation(vT0[:, (b - SV) % 2, :], proj[u % 2][:], ACT.Copy
                                                 ).then_inc(proj_free[u % 2], 1)
                        elif SK <= b:
                            nc.scalar.activation(k_sb[:, b - SK, :], proj[u % 2][:], ACT.Copy
                                                 ).then_inc(proj_free[u % 2], 1)
                        else:
                            nc.scalar.activation(q_sb[:, b, :], proj[u % 2][:], ACT.Copy, scale=HEAD ** -0.5
                                                 ).then_inc(proj_free[u % 2], 1)
                    u += 1
                elif kind == "A":
                    if b:
                        act.wait_ge(sp_done, 4 * b)
                    for j in range(TB):
                        act.wait_ge(z_full, 4 * b + j + 1)
                        nc.scalar.activation(soft_a[:, Z_OFF[j]:Z_OFF[j] + Z_LEN[j]], zb[j][:, 0:Z_LEN[j]],
                                             ACT.Abs).then_inc(abs_done, 1)
                    act.wait_ge(abs_done, 4 * b + 4)
                    link(nc.scalar.activation(soft_a[:], soft_a[:], ACT.Exp, scale=-1.0))
                    nc.scalar.activation(soft_a[:], soft_a[:], ACT.Ln, bias=1.0).then_inc(log_done, 1)
                    if b:
                        act.wait_ge(cum_full, 4 * b)
                    for j in range(TB):
                        at = slice(Z_OFF[j], Z_OFF[j] + Z_LEN[j])
                        act.wait_ge(sp_sum, 4 * b + j + 1)
                        nc.scalar.activation(softplus[:, 0, at], soft_a[:, at], ACT.Copy).then_inc(sp_hi, 1)
                elif kind == "B":
                    if b:
                        act.wait_ge(pv_done, b)
                    for j in range(TB):
                        act.wait_ge(cum_full, 4 * b + j + 1)
                        nc.scalar.activation(weights[:, Z_OFF[j]:Z_OFF[j] + Z_LEN[j]], zb[j][:, 0:Z_LEN[j]],
                                             ACT.Exp).then_inc(wt_done, 1)
                elif kind == "T":
                    act.wait_ge(misc_full, MISC_AT[f"V{b}"] + 1)
                    nc.scalar.activation(v_nat0[:, :, b * P:(b + 1) * P],
                                         misc[:].rearrange("p (t n) -> p t n", t=TB), ACT.Copy
                                         ).then_inc(misc_free, 1)

            def window_exp(h):
                s = h % 3
                act.wait_ge(max_done, h + 1)
                if h < 3:
                    act.wait_ge(pv_done, SB_HEADS)
                else:
                    act.wait_ge(pt_full, 2 * h - 4)
                for b in range(TB):
                    z, lo, at, n = window_block(b, s)
                    nc.scalar.activation(p_bufs[s][:, at:at + n], z[:, lo:lo + n], ACT.Exp,
                                         bias=soft[:, s, 0, b:b + 1], accum_out=soft[:, s, 1, b:b + 1])
                nc.scalar.activation(soft[:, s, 2, :], soft[:, s, 0, :], ACT.Exp, bias=sinks[:, h:h + 1]
                                     ).then_inc(p_done, 1)

            def window_copy(h):
                act.wait_ge(pt_full, 2 * h + 1)
                if h >= 3:
                    act.wait_ge(pv_done, SB_HEADS + h - 2)
                nc.scalar.activation(pt_bufs[h % 3][:, 0:384], pairs[h % 3][0][:, 0:384], ACT.Copy
                                     ).then_inc(pt_act, 1)

            window_exp(0)
            window_exp(1)
            for h in range(SW_HEADS):
                window_copy(h)
                if h + 2 < SW_HEADS:
                    window_exp(h + 2)
            heads_hi("o0", oT0, lambda dc: act.wait_ge(o_free, dc + 1))

            def out_units(u0, n):
                for o in range(DC):
                    if o < DC - 1:
                        split(u0 + o + 2, o % 2)
                    squares(n, o)
                split(u0 + DC + 1, 1)
                root(n)
                modulated(n)

            def ffn(layer, u0, base):
                act.preload_act_table_set(GELU_SET)
                with act.Fori(0, FB) as f:
                    u = u0 + 2 * f
                    split(u + 2, 0)
                    act.wait_ge(unit_mm, u + 1)
                    nc.scalar.activation(normed[:, 0, 2:2 + SEQ], proj[0][:], ACT.Copy
                                         ).then_inc(proj_free[0], 1)
                    act.wait_ge(conv_done, base + f + 1)
                    nc.scalar.activation(square[:, 1, :], square[:, 0, :], ACT.Gelu_apprx_tanh,
                                         bias=conv_col(layer, 3, f)).then_inc(gelu_done, 1)
                    split(u + 3, 1)
                    act.wait_ge(gp_done, base + f + 2)
                    nc.scalar.activation(gated_hi[layer][:, bass.ds(f, 1), :].rearrange("p a n -> p (a n)"),
                                         h32[:, 0, :], ACT.Copy).then_inc(gp_hi, 1)

            def down(u0, n, last=False):
                act.preload_act_table_set(EXP_LN_SET)
                with act.Fori(0, HALF // 2) as i:
                    for s in range(2):
                        split(u0 + 2 * i + (2 + s), s)
                for q in range(4):
                    squares(n, q)
                split(u0 + HALF + 1, 0)
                split(u0 + HALF + 2, 1)
                with act.Fori(0, HALF // 2 - 1) as i:
                    for s in range(2):
                        split(u0 + HALF + 3 + 2 * i + s, s)
                for q in range(4, DC):
                    squares(n, q)
                if not last:
                    split(u0 + FB, 0)
                    split(u0 + FB + 1, 1)
                root(n)
                if not last:
                    modulated(n)

            out_units(U_OUT0, 1)
            ffn(0, U_FFN0, 0)
            down(U_DOWN0, 2)

            def sigmoid_of_minus(t):
                link(nc.scalar.activation(t, t, ACT.Exp))
                link(nc.scalar.activation(t, t, ACT.Ln, bias=1.0))
                return nc.scalar.activation(t, t, ACT.Exp, scale=-1.0)

            u = U_IN1
            f_tile, g_tile = normed[:, 0, 2:2 + SEQ], normed[:, 1, 2:2 + SEQ]
            for h in range(HG_HEADS + 2):
                p, o = h - 1, h - 2
                if h < HG_HEADS:
                    split(u + 2, 0)
                    act.wait_ge(unit_mm, u + 1)
                if h > 1:
                    act.wait_ge(misc_full, MISC_AT[f"osq{o}"] + 1)
                    if o:
                        act.wait_ge(ho_done, o)
                    nc.scalar.activation(square[:, 1, :], misc[:], ACT.Ln, bias=EPS, scale=1.0 / P
                                         ).then_inc(misc_free, 1)
                    act.wait_ge(misc_free, MISC_AT[f"osq{o}"] + 1)
                    nc.scalar.activation(square[:, 1, :], square[:, 1, :], ACT.Exp, scale=-0.5
                                         ).then_inc(orstd_done, 1)
                if 0 < h <= HG_HEADS:
                    act.wait_ge(misc_full, MISC_AT[f"val{p}"] + 1)
                if h < HG_HEADS:
                    nc.scalar.activation(vT1[:], proj[0][:], ACT.Copy).then_inc(proj_free[0], 1)
                if 0 < h <= HG_HEADS:
                    nc.scalar.activation(v_nat1[:], misc[:].rearrange("p (t n) -> p t n", t=TB), ACT.Copy
                                         ).then_inc(misc_free, 1)
                    act.wait_ge(misc_full, MISC_AT[f"key{p}"] + 1)
                    nc.scalar.activation(key_nat[:], misc[:, 0:384].rearrange("p (t n) -> p t n", t=3),
                                         ACT.Copy).then_inc(misc_free, 1)
                if h < HG_HEADS:
                    split(u + 3, 1)
                    act.wait_ge(f_clamped, h + 1)
                    sigmoid_of_minus(f_tile).then_inc(fexp_done, 1)
                    act.wait_ge(f_ready, h + 1)
                    nc.scalar.activation(f_tile, k_hg[:], ACT.Ln, bias=1.0, scale=-1.0).then_inc(logf_done, 1)
                    split(u + 4, 0)
                    act.wait_ge(unit_mm, u + 3)
                    if h:
                        act.wait_ge(lq_done, p + 1)
                    nc.scalar.activation(q_hg[:], proj[0][:], ACT.Copy).then_inc(proj_free[0], 1)
                    act.wait_ge(cum_done, h + 1)
                    nc.scalar.activation(decay[:], cum[:], ACT.Exp).then_inc(dec_done, 1)
                    for part, ready in enumerate((diff_dve, diff_pool)):
                        act.wait_ge(ready, h + 1)
                        e = level_e[:, 4 * part:4 * part + 4, :]
                        nc.scalar.activation(e, e, ACT.Exp).then_inc(level_exp, 1)
                    split(u + 5, 1)
                    act.wait_ge(g_clamped, h + 1)
                    sigmoid_of_minus(g_tile).then_inc(gexp_done, 1)
                if 0 < h <= HG_HEADS:
                    act.wait_ge(ho_full, p + 1)
                    if p:
                        act.wait_ge(misc_full, MISC_AT[f"osq{p - 1}"] + 1)
                    nc.scalar.activation(square[:, 0, :], obank[:], ACT.Square).then_inc(osq_done, 1)
                u += 4
            heads_hi("o1", oT1, lambda dc: act.wait_ge(ho_done, dc + 1))
            out_units(U_OUT1, 3)
            ffn(1, U_FFN1, FB)
            down(U_DOWN1, 4, last=True)

            for dc in range(DC):
                act.wait_ge(fin_full, dc + 1)
                nc.scalar.activation(out_nat[:, :, dc * P:(dc + 1) * P],
                                     zb[dc % 4][:].rearrange("p (t n) -> p t n", t=TB), ACT.Copy
                                     ).then_inc(fin_evac, 1)

        @block.vector
        def _(dve):
            chain = [0]

            def link(ins):
                chain[0] += 1
                ins.then_inc(dve_chain, 1)
                dve.wait_ge(dve_chain, chain[0])

            def split(u, slot):
                dve.wait_ge(hi_done, u + 1)
                nc.vector.tensor_tensor(w_lo[:, slot, :], w_raw[:, slot, :], w_hi[:, slot, :].bitcast(F32),
                                        ALU.subtract).then_inc(lo_done, 1)

            def add_squares(n, dc):
                if 0 < dc < DC - 1:
                    dve.wait_ge(sq_done, 8 * n + dc + 1)
                    if 6 * n + dc - 1:
                        dve.wait_ge(ss_done, 6 * n + dc - 1)
                    nc.vector.tensor_tensor(sumsq[:], sumsq[:], square[:, dc % 2, :], ALU.add).then_inc(ss_done, 1)

            def normalise(n):
                base = h_base[f"norm{n}"]
                shift = mod[:, 6 * (n // 2) + 3 * (n % 2), :]
                dve.wait_ge(rstd_done, n + 1)
                dve.wait_ge(mod_ready, n + 1)
                for dc in range(DC + 1):
                    if dc < DC:
                        if dc >= 2:
                            dve.wait_ge(h_lo, base + dc - 1)
                        nc.vector.scalar_tensor_tensor(out=normed[:, dc % 2, 2:2 + SEQ], in0=xT[:, dc, :],
                                                       scalar=scale_g[:, n, dc:dc + 1], in1=rstd[:],
                                                       op0=ALU.mult, op1=ALU.mult).then_inc(normed_done, 1)
                    if dc:
                        d = dc - 1
                        dve.wait_ge(h_hi, base + d + 1)
                        nc.vector.scalar_tensor_tensor(out=hT_lo[:, d, :], in0=normed[:, d % 2, 2:2 + SEQ],
                                                       scalar=shift[:, d:d + 1], in1=hT_hi[:, d, :].bitcast(F32),
                                                       op0=ALU.add, op1=ALU.subtract).then_inc(h_lo, 1)

            def low(base, dc, src):
                dve.wait_ge(h_hi, base + dc + 1)
                nc.vector.tensor_tensor(hT_lo[:, dc, :], src, hT_hi[:, dc, :].bitcast(F32), ALU.subtract
                                        ).then_inc(h_lo, 1)

            def mod_group(g):
                dve.wait_ge(misc_full, MISC_AT[f"mod{g}"] + 1)
                nc.vector.tensor_tensor(mod[:, g, :], misc[:, 0:DC], bias_col[:, g * DC:(g + 1) * DC], ALU.add
                                        ).then_inc(misc_free, 1)
                dve.wait_ge(misc_free, MISC_AT[f"mod{g}"] + 1)
                if g % 3 == 1:
                    nc.vector.scalar_tensor_tensor(out=scale_g[:, g // 3, :], in0=mod[:, g, :], scalar=1.0,
                                                   in1=norm_g[g // 3], op0=ALU.add, op1=ALU.mult
                                                   ).then_inc(mod_ready, 1)

            dve.wait_ge(small_in, 16 * 11)
            dve.wait_ge(const_in, 48)
            for i in range(4):
                dve.wait_ge(misc_full, MISC_AT[f"small{i}"] + 1)
                nc.vector.tensor_copy(small[:, i, :], misc[:, 0:96]).then_inc(misc_free, 1)
            dve.wait_ge(misc_free, 4)
            nc.vector.tensor_copy(ident_r[:], ident).then_inc(gp_done, 1)
            nc.vector.tensor_copy(table_r[:], table2).then_inc(small_ready, 1)
            nc.vector.memset(normed[:, 0, 0:2], 0.0).then_inc(small_ready, 1)
            nc.vector.tensor_tensor(lower[:, 0, :], gamma[0], gamma[1], ALU.subtract).then_inc(small_ready, 1)
            dve.wait_ge(cond_exp, 1)
            link(nc.vector.tensor_scalar(cond[:, 1, :], cond[:, 0, :], 1.0, None, ALU.add))
            link(nc.vector.reciprocal(cond[:, 0, :], cond[:, 1, :]))
            nc.vector.tensor_tensor(cond[:, 2, :], c_col, cond[:, 0, :], ALU.mult).then_inc(cond_ready, 1)
            link(nc.vector.tensor_scalar(lower[:, 0, :], lower[:, 1, :], 1.0, None, ALU.add))
            link(nc.vector.reciprocal(lower[:, 1, :], lower[:, 0, :]))
            link(nc.vector.tensor_scalar(lower[:, 2, :], lower[:, 1, :], -1.0, 1.0, ALU.mult, ALU.add))
            for h in range(SW_HEADS):
                nc.vector.tensor_scalar(slope_r[:, h, :], ident, 2.0 ** (-8.0 * (h + 1) / SW_HEADS), None,
                                        ALU.mult).then_inc(tables_ready, 1)

            dve.wait_ge(cond_ready, 1)

            def ada_block(j):
                g, k = divmod(j, DC)
                dve.wait_ge(ada_first_in[j // 4], 16)
                acc, raw, scale = ada_sum[:, g, :], ada_first[:, j // 4, j % 4, :], cond[:, 2, k:k + 1]
                if k == 0:
                    nc.vector.tensor_scalar(acc, raw, scale, None, ALU.mult).then_inc(ada_used, 1)
                else:
                    dve.wait_ge(ada_used, j)
                    nc.vector.scalar_tensor_tensor(out=acc, in0=raw, scalar=scale, in1=acc, op0=ALU.mult,
                                                   op1=ALU.add).then_inc(ada_used, 1)

            def x_block(dc):
                dve.wait_ge(xt_full, dc + 1)
                nc.vector.tensor_copy(xT[:, dc, :], zb[dc % 4][:]).then_inc(x_new, 1)

            for dc in range(DC):
                x_block(dc)
                if dc:
                    add_squares(0, dc - 1)
            add_squares(0, DC - 1)
            for j in range(2 * DC):
                ada_block(j)
            split(0, 0)
            split(1, 1)
            mod_group(0)
            mod_group(1)
            normalise(0)

            u = 0
            for kind, b in STEPS0:
                if kind == "u":
                    split(u + 2, u % 2)
                    if b >= WQ:
                        dve.wait_ge(unit_mm, u + 1)
                        src = proj[u % 2]
                        if b == WV:
                            dve.wait_ge(misc_full, MISC_AT["V0"] + 1)
                            nc.vector.tensor_copy(vT0[:, 0, :], src[:]).then_inc(proj_free[u % 2], 1)
                        elif b == WK:
                            for g in range(2):
                                for half in range(2):
                                    last = nc.vector.tensor_copy(
                                        k_sw[HEAD * half:HEAD * half + HEAD, g, :],
                                        src[HEAD * g:HEAD * g + HEAD, :])
                            last.then_inc(proj_free[u % 2], 1)
                        else:
                            nc.vector.tensor_scalar(q_sw[:, b - WQ, :], src[:], HEAD ** -0.5, None, ALU.mult
                                                    ).then_inc(proj_free[u % 2], 1)
                    u += 1
                elif kind == "A":
                    dve.wait_ge(log_done, b + 1)
                    for j in range(TB):
                        at = slice(Z_OFF[j], Z_OFF[j] + Z_LEN[j])
                        nc.vector.scalar_tensor_tensor(out=soft_a[:, at], in0=zb[j][:, 0:Z_LEN[j]],
                                                       scalar=0.0, in1=soft_a[:, at], op0=ALU.max, op1=ALU.add
                                                       ).then_inc(sp_sum, 1)
                    for j in range(TB):
                        at = slice(Z_OFF[j], Z_OFF[j] + Z_LEN[j])
                        dve.wait_ge(sp_hi, 4 * b + j + 1)
                        nc.vector.tensor_tensor(softplus[:, 1, at], soft_a[:, at],
                                                softplus[:, 0, at].bitcast(F32), ALU.subtract
                                                ).then_inc(sp_done, 1)
                elif kind == "C" and b % 2:
                    dve.wait_ge(pv_done, b + 1)
                    nc.vector.tensor_copy(oT0[:, b // 2, :], obank[:]).then_inc(o_free, 1)

            def window_max(h):
                s = h % 3
                for b in range(TB):
                    z, lo, _, n = window_block(b, s)
                    dve.wait_ge(sw_full, 2 * h + 1 + b // 2)
                    link(nc.vector.tensor_reduce(soft[:, s, 3, b:b + 1], z[:, lo:lo + n], AX.X, ALU.max))
                nc.vector.tensor_scalar(soft[:, s, 0, :], soft[:, s, 3, :], sinks[:, h:h + 1], -1.0,
                                        ALU.max, ALU.mult).then_inc(max_done, 1)

            def window_norm(h):
                s = h % 3
                dve.wait_ge(p_done, h + 1)
                link(nc.vector.tensor_tensor(soft[:, s, 3, :], soft[:, s, 1, :], soft[:, s, 2, :], ALU.add))
                link(nc.vector.reciprocal(soft[:, s, 2, :], soft[:, s, 3, :]))
                for b in range(TB):
                    _, _, at, n = window_block(b, s)
                    nc.vector.tensor_scalar(p_bufs[s][:, at:at + n], p_bufs[s][:, at:at + n],
                                            soft[:, s, 2, b:b + 1], None, ALU.mult).then_inc(p_norm, 1)

            def window_copy(h):
                dve.wait_ge(pt_full, 2 * h + 2)
                if h >= 3:
                    dve.wait_ge(pv_done, SB_HEADS + h - 2)
                nc.vector.tensor_copy(pt_bufs[h % 3][:, 384:896], pairs[h % 3][1][:]).then_inc(pt_dve, 1)

            def window_out(h):
                dve.wait_ge(pv_done, SB_HEADS + h + 1)
                nc.vector.tensor_copy(oT0[:, 4 + h // 2, :], obank[:]).then_inc(o_free, 1)

            window_max(0)
            window_max(1)
            window_norm(0)
            for h in range(SW_HEADS):
                window_copy(h)
                if h + 1 < SW_HEADS:
                    window_norm(h + 1)
                if h + 2 < SW_HEADS:
                    window_max(h + 2)
                if 2 <= h < 6:
                    mod_group(h)
                if h % 2 == 0 and h:
                    window_out(h - 1)
            window_out(SW_HEADS - 1)
            for dc in range(DC):
                low(h_base["o0"], dc, oT0[:, dc, :])

            def out_units(u0, n, gate):
                for o in range(DC):
                    if o < DC - 1:
                        split(u0 + o + 2, o % 2)
                    dve.wait_ge(unit_mm, u0 + o + 1)
                    nc.vector.scalar_tensor_tensor(out=xT[:, o, :], in0=proj[o % 2][:],
                                                   scalar=mod[:, gate, o:o + 1], in1=xT[:, o, :],
                                                   op0=ALU.mult, op1=ALU.add).then_inc(x_new, 1)
                    add_squares(n, o)
                split(u0 + DC + 1, 1)
                normalise(n)

            def ffn(layer, u0, base):
                lc = chain[0]
                with dve.Fori(0, FB) as f:
                    u = u0 + 2 * f
                    split(u + 2, 0)
                    dve.wait_ge(proj_free[0], FREE0_FFN[layer] + f + 1)
                    nc.vector.tensor_scalar(square[:, 0, :], normed[:, 0, 0:SEQ], conv_col(layer, 0, f), None,
                                            ALU.mult).then_inc(dve_chain, 1)
                    dve.wait_ge(dve_chain, lc + 2 * f + 1)
                    nc.vector.scalar_tensor_tensor(out=square[:, 0, :], in0=normed[:, 0, 1:1 + SEQ],
                                                   scalar=conv_col(layer, 1, f), in1=square[:, 0, :],
                                                   op0=ALU.mult, op1=ALU.add).then_inc(dve_chain, 1)
                    dve.wait_ge(dve_chain, lc + 2 * f + 2)
                    nc.vector.scalar_tensor_tensor(out=square[:, 0, :], in0=normed[:, 0, 2:2 + SEQ],
                                                   scalar=conv_col(layer, 2, f), in1=square[:, 0, :],
                                                   op0=ALU.mult, op1=ALU.add).then_inc(conv_done, 1)
                    dve.wait_ge(unit_mm, u + 2)
                    dve.wait_ge(gelu_done, base + f + 1)
                    nc.vector.tensor_tensor(h32[:, 0, :], proj[1][:], square[:, 1, :], ALU.mult
                                            ).then_inc(gp_done, 1)
                    split(u + 3, 1)
                    dve.wait_ge(gp_hi, base + f + 1)
                    at = gated_lo[layer][:, bass.ds(f, 1), :].rearrange("p a n -> p (a n)")
                    hi = gated_hi[layer][:, bass.ds(f, 1), :].rearrange("p a n -> p (a n)")
                    nc.vector.tensor_tensor(at, h32[:, 0, :], hi.bitcast(F32), ALU.subtract
                                            ).then_inc(gp_lo, 1)
                chain[0] += 2 * FB

            def down(u0, n, gate, last=False):
                def half_out(half, u):
                    for q in range(4):
                        dc = 4 * half + q
                        if q < 3:
                            dve.wait_ge(down_full, 3 * (n - 2 + half) + q + 1)
                        else:
                            dve.wait_ge(unit_mm, u)
                        nc.vector.scalar_tensor_tensor(out=xT[:, dc, :], in0=zb[q][:],
                                                       scalar=mod[:, gate, dc:dc + 1], in1=xT[:, dc, :],
                                                       op0=ALU.mult, op1=ALU.add).then_inc(x_new, 1)
                        if q:
                            add_squares(n, dc - 1)
                    add_squares(n, dc)

                if n == 2:
                    mod_group(6)
                    mod_group(7)
                with dve.Fori(0, HALF // 2) as i:
                    for s in range(2):
                        split(u0 + 2 * i + (2 + s), s)
                half_out(0, u0 + HALF)
                split(u0 + HALF + 1, 0)
                split(u0 + HALF + 2, 1)
                with dve.Fori(0, HALF // 2 - 1) as i:
                    for s in range(2):
                        split(u0 + HALF + 3 + 2 * i + s, s)
                half_out(1, u0 + FB)
                if not last:
                    split(u0 + FB, 0)
                    split(u0 + FB + 1, 1)

            out_units(U_OUT0, 1, 2)
            ffn(0, U_FFN0, 0)
            down(U_DOWN0, 2, 5)
            normalise(2)

            nc.vector.memset(starts[:], 1.0).then_inc(tables_ready, 1)
            dve.wait_ge(tables_ready, SW_HEADS + 1)
            link(nc.vector.memset(starts[:].rearrange("p (t n) -> p t n", t=TB)[:, :, 0:1], 0.0))
            u = U_IN1
            f_tile, g_tile = normed[:, 0, 2:2 + SEQ], normed[:, 1, 2:2 + SEQ]
            for h in range(HG_HEADS + 2):
                p, o = h - 1, h - 2
                if h < HG_HEADS:
                    split(u + 2, 0)
                if 0 < h <= HG_HEADS:
                    dve.wait_ge(gexp_done, p + 1)
                    nc.vector.tensor_tensor(gate_o[:, p % 2, :], proj[1][:], g_tile, ALU.mult).then_inc(g_done, 1)
                if h < HG_HEADS:
                    split(u + 3, 1)
                    dve.wait_ge(unit_mm, u + 2)
                    nc.vector.tensor_scalar(f_tile, proj[1][:], CLAMP, None, ALU.min).then_inc(f_clamped, 1)
                if h > 1:
                    dve.wait_ge(orstd_done, o + 1)
                    nc.vector.tensor_tensor(square[:, 1, :], obank[:], square[:, 1, :], ALU.mult
                                            ).then_inc(ho_free, 1)
                    dve.wait_ge(ho_free, o + 1)
                    nc.vector.scalar_tensor_tensor(out=oT1[:, o, :], in0=square[:, 1, :], scalar=onorm,
                                                   in1=gate_o[:, o % 2, :], op0=ALU.mult, op1=ALU.mult
                                                   ).then_inc(ho_done, 1)
                if 0 < h <= HG_HEADS:
                    dve.wait_ge(misc_full, MISC_AT[f"diag{p}"] + 1)
                    nc.vector.tensor_tensor(
                        scores[:].rearrange("p (t n) -> p t n", t=TB), misc[:].rearrange("p (t n) -> p t n", t=TB),
                        ident.unsqueeze(1).to_broadcast([P, TB, P]), ALU.mult).then_inc(misc_free, 1)
                    dve.wait_ge(misc_free, MISC_AT[f"diag{p}"] + 1)
                    dve.wait_ge(lev_full, p + 1)
                    dve.wait_ge(masks_in, 16)
                    for j in range(LEVELS):
                        half = 1 << j
                        dst = scores[:].rearrange("p (b two r) -> p b two r", two=2, r=half)[:, :, 1, :]
                        src = zb[j // 2][:, 256 * (j % 2):256 * (j % 2) + 256].rearrange("p (b r) -> p b r", r=half)
                        m = masks[:, j, :].bitcast(U32).rearrange("p (b r) -> p b r", r=half)
                        if LEVELS * p + j:
                            dve.wait_ge(score_done, LEVELS * p + j)
                        nc.vector.copy_predicated(dst, m, src).then_inc(score_done, 1)
                    dve.wait_ge(misc_full, MISC_AT[f"kv{p}"] + 1)
                    link(nc.vector.tensor_copy(states[:, 0, :], misc[:, 0:P]))
                    link(nc.vector.scalar_tensor_tensor(
                        out=states[:, 1, :], in0=states[:, 0, :], scalar=last_dec[:, p % 2, 1:2],
                        in1=misc[:, P:2 * P], op0=ALU.mult, op1=ALU.add))
                    nc.vector.scalar_tensor_tensor(
                        out=states[:, 2, :], in0=states[:, 1, :], scalar=last_dec[:, p % 2, 2:3],
                        in1=misc[:, 2 * P:3 * P], op0=ALU.mult, op1=ALU.add).then_inc(misc_free, 1)
                if h < HG_HEADS:
                    dve.wait_ge(fexp_done, h + 1)
                    if h:
                        dve.wait_ge(lk_done, (LEVELS + 1) * h)
                        dve.wait_ge(lev_full, h)
                    nc.vector.tensor_scalar(k_hg[:], f_tile, lower[:, 2, h:h + 1], BELOW_ONE, ALU.mult, ALU.min
                                            ).then_inc(f_ready, 1)
                    dve.wait_ge(logf_done, h + 1)
                    if h:
                        dve.wait_ge(dec_done, h)
                        dve.wait_ge(diff_pool, h)
                    nc.vector.tensor_tensor_scan(cum[:], starts[:], f_tile, 0.0, ALU.mult, ALU.add
                                                 ).then_inc(cum_done, 1)
                    dve.wait_ge(cum_done, h + 1)
                    for j in range(4):
                        a, b, mid, to_mid, from_mid = level_views(j)
                        nc.vector.tensor_tensor(to_mid, mid, a, ALU.subtract)
                        last = nc.vector.tensor_tensor(from_mid, b, mid, ALU.subtract)
                    last.then_inc(diff_dve, 1)
                    split(u + 4, 0)
                    dve.wait_ge(proj_free[0], FREE0_IN1 + 2 * h + 2)
                    dve.wait_ge(dec_done, h + 1)
                    nc.vector.tensor_tensor(q_dec[:, h % 2, :], q_hg[:], decay[:], ALU.mult)
                    nc.vector.tensor_copy(last_dec[:, h % 2, :],
                                          decay[:].rearrange("p (t n) -> p t n", n=P)[:, :, P - 1])
                    for j in range(LEVELS):
                        half = 1 << j
                        dve.wait_ge(level_exp, 2 * h + 1 + j // 4)
                        e = level_e[:, j, :].rearrange("p (b two r) -> p b two r", two=2, r=half)[:, :, 1, :]
                        qv = q_hg[:].rearrange("p (b two r) -> p b two r", two=2, r=half)[:, :, 1, :]
                        last = nc.vector.tensor_tensor(
                            level_q[:, j, :].rearrange("p (b r) -> p b r", r=half), e, qv, ALU.mult)
                    last.then_inc(lq_done, 1)
                    split(u + 5, 1)
                    dve.wait_ge(unit_mm, u + 4)
                    nc.vector.tensor_scalar(g_tile, proj[1][:], -1.0, CLAMP, ALU.mult, ALU.min
                                            ).then_inc(g_clamped, 1)
                if 1 <= h <= 4:
                    mod_group(7 + h)
                u += 4
            for dc in range(DC):
                low(h_base["o1"], dc, oT1[:, dc, :])
            out_units(U_OUT1, 3, 8)
            ffn(1, U_FFN1, FB)
            down(U_DOWN1, 4, 11, last=True)

            dve.wait_ge(rstd_done, 5)
            for dc in range(DC):
                if dc >= 2:
                    dve.wait_ge(fin_full, dc - 1)
                nc.vector.scalar_tensor_tensor(out=h32[:, dc % 2, :], in0=xT[:, dc, :],
                                               scalar=fin_g[:, dc:dc + 1], in1=rstd[:],
                                               op0=ALU.mult, op1=ALU.mult).then_inc(fin_y, 1)

        @block.tensor
        def _(pe):
            def mm(dst, weights_ap, moving, start=False, stop=False):
                return nc.tensor.matmul(dst, weights_ap, moving, start=start, stop=stop,
                                        skip_group_check=True)

            def misc_wait(name):
                if MISC_AT[name]:
                    pe.wait_ge(misc_free, MISC_AT[name])

            def parts_ready(u):
                pe.wait_ge(hi_done, u + 1)
                pe.wait_ge(lo_done, u + 1)

            def unit(u, slot, dst, h_from=None):
                parts_ready(u)
                for k in range(DC):
                    if h_from is not None:
                        pe.wait_ge(h_lo, h_from + k + 1)
                    at = slice(k * P, (k + 1) * P)
                    mm(dst, w_hi[:, slot, at], hT_hi[:, k, :], start=(k == 0))
                    mm(dst, w_hi[:, slot, at], hT_lo[:, k, :])
                    last = mm(dst, w_lo[:, slot, at], hT_hi[:, k, :], stop=(k == DC - 1))
                last.then_inc(unit_mm, 1)

            def unit_pair(u, h_from):
                parts_ready(u + 1)
                for k in range(DC):
                    pe.wait_ge(h_lo, h_from + k + 1)
                    at = slice(k * P, (k + 1) * P)
                    for s in range(2):
                        mm(proj[s][:], w_hi[:, s, at], hT_hi[:, k, :], start=(k == 0))
                        mm(proj[s][:], w_hi[:, s, at], hT_lo[:, k, :])
                        last = mm(proj[s][:], w_lo[:, s, at], hT_hi[:, k, :], stop=(k == DC - 1))
                        if k == DC - 1:
                            last.then_inc(unit_mm, 1)

            def norm_sum(n):
                pe.wait_ge(ss_done, 6 * n + 6)
                misc_wait(f"norm{n}")
                mm(misc[:], ones, sumsq[:], start=True)
                pe.wait_ge(sq_done, 8 * n + 8)
                mm(misc[:], ones, square[:, 1, :], stop=True).then_inc(misc_full, 1)

            def mod_sum(g):
                if g < 2:
                    pe.wait_ge(ada_used, DC * (g + 1))
                else:
                    pe.wait_ge(sum_pool, (DC - 1) * (g - 1))
                misc_wait(f"mod{g}")
                for dc in range(DC):
                    last = mm(misc[:, dc:dc + 1], ada_sum[:, g % 4, dc * P:(dc + 1) * P], ones[:, 0:1],
                              True, True)
                last.then_inc(misc_full, 1)

            pe.wait_ge(const_in, 48)
            pe.wait_ge(small_in, 16 * 11)
            for i, n in enumerate((96, 96, 96, 96)):
                misc_wait(f"small{i}")
                nc.tensor.transpose(misc[:, 0:n], small_nat[0:n, i, :], ident[0:n, 0:n]).then_inc(misc_full, 1)
            pe.wait_ge(x_in, 16)
            for dc in range(DC):
                if dc >= 4:
                    pe.wait_ge(x_new, dc - 3)
                for t in range(TB):
                    last = nc.tensor.transpose(zb[dc % 4][:, t * P:(t + 1) * P],
                                               x_nat[:, t, dc * P:(dc + 1) * P], ident)
                last.then_inc(xt_full, 1)
            norm_sum(0)
            mod_sum(0)
            mod_sum(1)

            def tile_in(b):
                n = UNITS0.index(b)
                pe.wait_ge(proj_free[n % 2], n // 2 + 1)

            pe.wait_ge(tables_ready, SW_HEADS)
            u = 0
            for kind, b in STEPS0:
                if kind == "u":
                    if u >= 2:
                        pe.wait_ge(proj_free[u % 2], u // 2)
                        unit(u, u % 2, proj[u % 2][:])
                    elif u == 0:
                        unit_pair(0, h_base["norm0"])
                    u += 1
                elif kind == "T":
                    tile_in(SV + b)if b < 4 else tile_in(WV)
                    misc_wait(f"V{b}")
                    for t in range(TB):
                        last = nc.tensor.transpose(misc[:, t * P:(t + 1) * P],
                                                   vT0[:, b % 2, t * P:(t + 1) * P], ident)
                    last.then_inc(misc_full, 1)
                elif kind == "A":
                    hp, r = b // 2, slice(HEAD * (b % 2), HEAD * (b % 2) + HEAD)
                    tile_in(SQ + hp)
                    tile_in(SK + hp)
                    for j in range(TB):
                        if b:
                            pe.wait_ge(wt_done, 4 * (b - 1) + j + 1)
                        mm(zb[j][:, 0:Z_LEN[j]], k_sb[r, hp, j * P:(j + 1) * P], q_sb[r, hp, j * P:SEQ],
                           start=True)
                        mm(zb[j][:, 0:P], ident_r[:], strict_r, stop=True).then_inc(z_full, 1)
                elif kind == "B":
                    pe.wait_ge(sp_done, 4 * b + 4)
                    for j in range(TB):
                        for part in range(2):
                            own = softplus[:, part, Z_OFF[j]:Z_OFF[j] + Z_LEN[j]]
                            last = mm(zb[j][:, 0:Z_LEN[j]], suffix, own, stop=(part == 1 and j == TB - 1))
                        for j2 in range(j + 1, TB):
                            for part in range(2):
                                last = mm(zb[j][:, (j2 - j) * P:Z_LEN[j]], minus,
                                          softplus[:, part, Z_OFF[j2]:Z_OFF[j2] + Z_LEN[j2]],
                                          stop=(part == 1 and j2 == TB - 1))
                        last.then_inc(cum_full, 1)
                else:
                    hp, r = b // 2, slice(HEAD * (b % 2), HEAD * (b % 2) + HEAD)
                    pe.wait_ge(wt_done, 4 * b + 4)
                    pe.wait_ge(misc_free, MISC_AT[f"V{hp}"] + 1)
                    if b % 2 == 0 and hp:
                        pe.wait_ge(o_free, hp)
                    for j in range(TB):
                        last = mm(obank[r, j * P:SEQ], v_nat0[:, j, hp * P + r.start:hp * P + r.stop],
                                  weights[:, Z_OFF[j]:Z_OFF[j] + Z_LEN[j]], start=(j == 0), stop=(j == TB - 1))
                    last.then_inc(pv_done, 1)

            def window_logits(h):
                s, hp, g = h % 3, h // 2, h // SW_GROUP
                r = slice(HEAD * (h % 2), HEAD * (h % 2) + HEAD)
                tile_in(WQ + hp)
                if h == 2:
                    for bank_free in proj_free:
                        pe.wait_ge(bank_free, FREE_OUT0)
                if h >= 3:
                    pe.wait_ge(pt_act, h - 2)
                    pe.wait_ge(pt_dve, h - 2)
                for b in range(TB):
                    z, lo, _, n = window_block(b, s)
                    if b % 2 == 0:
                        first = P if b == 0 else 0
                        mm(z[:, 0:4 * P - first], slope_r[:, h, :], band_r[:, first:4 * P], start=True)
                    last = mm(z[:, lo:lo + n], q_sw[r, hp, b * P:(b + 1) * P],
                              k_sw[r, g, (b + 1) * P - n:(b + 1) * P], stop=True)
                    if b % 2:
                        last.then_inc(sw_full, 1)

            def window_transposes(h):
                pe.wait_ge(p_norm, 4 * h + 4)
                for i in range(7):
                    z, at = (pairs[h % 3][0], i) if i < 3 else (pairs[h % 3][1], i - 3)
                    last = nc.tensor.transpose(z[:, at * P:(at + 1) * P], p_bufs[h % 3][:, i * P:(i + 1) * P],
                                               ident)
                    if i in (2, 6):
                        last.then_inc(pt_full, 1)

            def window_values(h):
                s, g = h % 3, h // SW_GROUP
                r = slice(HEAD * (h % 2), HEAD * (h % 2) + HEAD)
                v_at = slice(4 * P + HEAD * g, 4 * P + HEAD * g + HEAD)
                pe.wait_ge(pt_act, h + 1)
                pe.wait_ge(pt_dve, h + 1)
                if h % 2 == 0:
                    pe.wait_ge(o_free, 4 + h // 2)
                for b in range(TB):
                    _, _, at, n = window_block(b, s)
                    blocks = [b] if b == 0 else [b - 1, b]
                    for i, kb in enumerate(blocks):
                        last = mm(obank[r, b * P:(b + 1) * P], v_nat0[:, kb, v_at],
                                  pt_bufs[s][:, at + i * P:at + (i + 1) * P], start=(b == 0), stop=(kb == b))
                last.then_inc(pv_done, 1)

            window_logits(0)
            window_logits(1)
            for h in range(SW_HEADS):
                window_transposes(h)
                if h:
                    window_values(h - 1)
                if h + 2 < SW_HEADS:
                    window_logits(h + 2)
                if 2 <= h < 6:
                    mod_sum(h)
            window_values(SW_HEADS - 1)

            def out_units(u0, n, base):
                for o in range(DC):
                    if o >= 2:
                        pe.wait_ge(x_new, 8 * n + o - 1)
                    elif n == 1:
                        pe.wait_ge(proj_free[o], FREE_OUT0)
                    else:
                        pe.wait_ge((proj_free[0], g_done)[o], (FREE0_FFN[1], HG_HEADS)[o])
                    unit(u0 + o, o % 2, proj[o % 2][:], base if o == 0 else None)
                norm_sum(n)

            def ffn(layer, u0, base, h_from):
                pe.wait_ge(proj_free[0], FREE0_FFN[layer])
                pe.wait_ge(gp_done, base + 1)
                unit_pair(u0, h_from)
                with pe.Fori(1, FB) as f:
                    pe.wait_ge(proj_free[0], FREE0_FFN[layer] + f)
                    unit(u0 + 2 * f, 0, proj[0][:])
                    pe.wait_ge(gp_done, base + f + 1)
                    unit(u0 + 2 * f + 1, 1, proj[1][:])

            def down(layer, u0, n):
                def one(u, slot, block, first=False):
                    parts_ready(u)
                    for k in range(2):
                        hi = gated_hi[layer][:, bass.ds(block + k, 1), :].rearrange("p a n -> p (a n)")
                        lo = gated_lo[layer][:, bass.ds(block + k, 1), :].rearrange("p a n -> p (a n)")
                        for q in range(4):
                            at = slice(k * 512 + q * P, k * 512 + (q + 1) * P)
                            if first and k == 0 and u > u0:
                                pe.wait_ge(x_new, 8 * n + q + 1)
                            mm(zb[q][:], w_hi[:, slot, at], hi, start=first and k == 0)
                            mm(zb[q][:], w_hi[:, slot, at], lo)
                            last = mm(zb[q][:], w_lo[:, slot, at], hi)
                    last.then_inc(unit_mm, 1)

                def last_two(u, slot, block):
                    for q, part in ((0, 0), (1, 0), (0, 1), (1, 1), (2, 0), (2, 1), (3, 0), (3, 1)):
                        if q == 0:
                            parts_ready(u + part)
                        sl = (slot + part) % 2
                        for k in range(2):
                            at = slice(k * 512 + q * P, k * 512 + (q + 1) * P)
                            i = 2 * part + k
                            hi, lo = gated_hi[layer][:, block + i, :], gated_lo[layer][:, block + i, :]
                            mm(zb[q][:], w_hi[:, sl, at], hi)
                            mm(zb[q][:], w_hi[:, sl, at], lo)
                            last = mm(zb[q][:], w_lo[:, sl, at], hi, stop=i == 3)
                        if q == 3:
                            last.then_inc(unit_mm, 1)
                        elif part == 1:
                            last.then_inc(down_full, 1)

                if layer == 0:
                    mod_sum(6)
                    mod_sum(7)
                pe.wait_ge(gp_lo, FB * (layer + 1))
                one(u0, 0, 0, first=True)
                one(u0 + 1, 1, 2)
                with pe.Fori(1, HALF // 2 - 1) as i:
                    for s in range(2):
                        one(u0 + 2 * i + s, s, 4 * i + 2 * s)
                one(u0 + HALF - 3, 0, FB - 6)
                last_two(u0 + HALF - 2, 1, FB - 4)
                one(u0 + HALF, 1, 0, first=True)
                with pe.Fori(0, HALF // 2 - 1) as i:
                    for s in range(2):
                        one(u0 + HALF + 1 + 2 * i + s, s, 4 * i + 2 * s + 2)
                last_two(u0 + FB - 2, 0, FB - 4)
                norm_sum(n)

            out_units(U_OUT0, 1, h_base["o0"])
            ffn(0, U_FFN0, 0, h_base["norm1"])
            down(0, U_DOWN0, 2)

            u = U_IN1
            for h in range(HG_HEADS + 2):
                p, o = h - 1, h - 2
                if h < HG_HEADS:
                    pe.wait_ge(proj_free[0], FREE0_IN1 + 2 * h)
                    if h == 0:
                        unit_pair(u, h_base["norm2"])
                    else:
                        unit(u, 0, proj[0][:])
                if h > 1:
                    pe.wait_ge(osq_done, o + 1)
                    misc_wait(f"osq{o}")
                    mm(misc[:], ones, square[:, 0, :], True, True).then_inc(misc_full, 1)
                if 0 < h <= HG_HEADS:
                    pe.wait_ge(proj_free[0], FREE0_IN1 + 2 * p + 1)
                    misc_wait(f"val{p}")
                    for t in range(TB):
                        last = nc.tensor.transpose(misc[:, t * P:(t + 1) * P], vT1[:, t * P:(t + 1) * P], ident)
                    last.then_inc(misc_full, 1)
                    pe.wait_ge(lk_done, (LEVELS + 1) * p + 1 + POOL_LEVELS.index(LEVELS))
                    misc_wait(f"key{p}")
                    for t in range(TB - 1):
                        last = nc.tensor.transpose(misc[:, t * P:(t + 1) * P],
                                                   level_k[:, LEVELS, t * P:(t + 1) * P], ident)
                    last.then_inc(misc_full, 1)
                if 0 < h < HG_HEADS:
                    pe.wait_ge(g_done, h)
                    unit(u + 1, 1, proj[1][:])
                if 0 < h <= HG_HEADS:
                    pe.wait_ge(lk_done, (LEVELS + 1) * (p + 1))
                    pe.wait_ge(lq_done, p + 1)
                    if p:
                        pe.wait_ge(score_done, LEVELS * p)
                    misc_wait(f"diag{p}")
                    for t in range(TB):
                        at = slice(t * P, (t + 1) * P)
                        last = mm(misc[:, at], k_hg[:, at], q_hg[:, at], True, True)
                    last.then_inc(misc_full, 1)
                    for j in range(LEVELS):
                        for t in range(TB):
                            lo = 256 * (j % 2) + 64 * t
                            last = mm(zb[j // 2][:, lo:lo + 64], level_k[:, j, t * P:(t + 1) * P],
                                      level_q[:, j, 64 * t:64 * t + 64], True, True)
                    last.then_inc(lev_full, 1)
                    misc_wait(f"kv{p}")
                    for t in range(TB - 1):
                        last = mm(misc[:, t * P:(t + 1) * P], key_nat[:, t, :], v_nat1[:, t, :], True, True)
                    last.then_inc(misc_full, 1)
                if h < HG_HEADS:
                    pe.wait_ge(proj_free[0], FREE0_IN1 + 2 * h + 1)
                    unit(u + 2, 0, proj[0][:])
                if 0 < h <= HG_HEADS:
                    pe.wait_ge(score_done, LEVELS * (p + 1))
                    pe.wait_ge(misc_free, MISC_AT[f"kv{p}"] + 1)
                    if p:
                        pe.wait_ge(ho_free, p)
                    for t in range(TB):
                        at = slice(t * P, (t + 1) * P)
                        last = mm(obank[:, at], v_nat1[:, t, :], scores[:, at], start=(t == 0), stop=(t == 0))
                        if t:
                            last = mm(obank[:, at], states[:, t - 1, :], q_dec[:, p % 2, at], stop=True)
                    last.then_inc(ho_full, 1)
                if h < HG_HEADS:
                    pe.wait_ge(f_clamped, h + 1)
                    unit(u + 3, 1, proj[1][:])
                if 1 <= h <= 4:
                    mod_sum(7 + h)
                u += 4
            out_units(U_OUT1, 3, h_base["o1"])
            ffn(1, U_FFN1, FB, h_base["norm3"])
            down(1, U_DOWN1, 4)

            for dc in range(DC):
                pe.wait_ge(fin_y, dc + 1)
                if dc >= 4:
                    pe.wait_ge(fin_evac, dc - 3)
                for t in range(TB):
                    last = nc.tensor.transpose(zb[dc % 4][:, t * P:(t + 1) * P],
                                               h32[:, dc % 2, t * P:(t + 1) * P], ident)
                last.then_inc(fin_full, 1)


_INS = ["x", "c", "ada_w", "ada_b", "norm_mix_g", "norm_ffn_g", "ab_w_in", "ab_sinks", "ab_w_out",
        "hg_w_in", "hg_lb_gamma", "hg_onorm_g", "hg_w_out", "ffn_w_gate", "ffn_w_up", "ffn_conv_w",
        "ffn_conv_b", "ffn_w_down", "final_g"]


def kernel(**inputs):
    import concourse.bacc as bacc
    from concourse.bass_utils import run_bass_kernel_spmd

    nc = bacc.Bacc("TRN2", target_bir_lowering=False, num_devices=1)
    arrays = {name: np.ascontiguousarray(inputs[name]) for name in _INS}
    arrays["tables"], levels = constant_tables()
    arrays["level_masks"] = levels.reshape(P, -1)
    args = [nc.dram_tensor(name, a.shape, mybir.dt.from_np(a.dtype), kind="ExternalInput").ap()
            for name, a in arrays.items()]
    result = nc.dram_tensor("result", (1, SEQ, D), F32, kind="ExternalOutput").ap()
    trunk(nc, *args, result)
    r = run_bass_kernel_spmd(nc, [arrays], core_ids=[0])
    return r.results[0]["result"]
```
